# Optimizing a Trainium2 kernel written in Bass

```python
import jax, jax.numpy as jnp
from jax import lax
import numpy as np

D_MODEL = 1024
BATCH = 1
SEQ = 256
DEPTH = 1
DEC_BATCH = 1
DEC_SEQ = 2048
PAST_LEN = 256

GRID_W = 64
MIX_GLA = 512
MIX_CONV = 512
GLA_HEADS = 4
GLA_DK = 64
GLA_DV = MIX_GLA // GLA_HEADS
GLA_KEY = GLA_HEADS * GLA_DK
GATE_RANK = 16
GATE_TAU = 16.0
CHUNK = 64
CONV_W = 31
N_EXPERTS = 16
EC_FACTOR = 2
D_EXPERT = 1024
EPS = 1e-6
IN_COLS = 2 * GLA_KEY + 2 * MIX_GLA + 2 * GATE_RANK + 2 * MIX_CONV

kernel_name = 'hymba_gla_conformer_ec_diffusion_step'

def _rmsnorm(x, g):
    xf = x.astype(jnp.float32)
    y = xf * lax.rsqrt(jnp.mean(xf * xf, axis=-1, keepdims=True) + EPS)
    return (y * g.astype(jnp.float32)).astype(x.dtype)

def _layernorm(x, g, b):
    xf = x.astype(jnp.float32)
    xc = xf - jnp.mean(xf, axis=-1, keepdims=True)
    y = xc * lax.rsqrt(jnp.mean(xc * xc, axis=-1, keepdims=True) + EPS)
    return (y * g.astype(jnp.float32) + b.astype(jnp.float32)).astype(x.dtype)

def _gla_scan(q, k, v, g, s0):
    b_, h_, t_, dk = q.shape
    dv = v.shape[-1]
    n = t_ // CHUNK
    q = q.reshape(b_, h_, n, CHUNK, dk)
    k = k.reshape(b_, h_, n, CHUNK, dk)
    v = v.reshape(b_, h_, n, CHUNK, dv)
    cum = jnp.cumsum(g.reshape(b_, h_, n, CHUNK, dk), axis=3)
    cum_last = cum[:, :, :, -1:, :]
    q_dec = q * jnp.exp(cum)
    k_inv = k * jnp.exp(-cum)
    lower = jnp.tril(jnp.ones((CHUNK, CHUNK), dtype=bool))
    scores = jnp.where(lower, jnp.einsum('bhnik,bhnjk->bhnij', q_dec, k_inv), 0.0)
    o_intra = jnp.einsum('bhnij,bhnjv->bhniv', scores, v)
    k_end = k * jnp.exp(cum_last - cum)
    upd = jnp.einsum('bhnck,bhncv->bhnkv', k_end, v)
    decay = jnp.exp(cum_last[:, :, :, 0, :])

    def step(s, inp):
        d, u = inp
        return d[..., None] * s + u, s

    s_fin, s_prev = lax.scan(step, s0, (jnp.moveaxis(decay, 2, 0), jnp.moveaxis(upd, 2, 0)))
    s_prev = jnp.moveaxis(s_prev, 0, 2)
    o_inter = jnp.einsum('bhnck,bhnkv->bhncv', q_dec, s_prev)
    return (o_intra + o_inter).reshape(b_, h_, t_, dv), s_fin

def _depthwise_conv(u, w, b):
    y = lax.conv_general_dilated(u, w[:, None, :], window_strides=(1,),
                                 padding=[(CONV_W // 2, CONV_W // 2)],
                                 dimension_numbers=('NWC', 'WIO', 'NWC'),
                                 feature_group_count=u.shape[-1])
    return y + b

def _mixer(h, grid, s0f, s0b, w_in, w_decay_f, b_decay_f, w_decay_b, b_decay_b,
           gla_norm_g, conv_w, conv_b, conv_ln_g, conv_ln_b, w_out):
    bsz, t, _ = h.shape
    proj = jnp.einsum('btd,dc->btc', h, w_in)
    o1 = GLA_KEY
    o2 = o1 + GLA_KEY
    o3 = o2 + MIX_GLA
    o4 = o3 + MIX_GLA
    o5 = o4 + GATE_RANK
    o6 = o5 + GATE_RANK
    o7 = o6 + MIX_CONV
    q, k, v, r, zf, zb, ga, gg = jnp.split(proj, [o1, o2, o3, o4, o5, o6, o7], axis=-1)

    def heads(a):
        return a.reshape(bsz, t, GLA_HEADS, -1).transpose(0, 2, 1, 3).astype(jnp.float32)

    gf = jax.nn.log_sigmoid((zf @ w_decay_f + b_decay_f).astype(jnp.float32)) / GATE_TAU
    gb = jax.nn.log_sigmoid((zb @ w_decay_b + b_decay_b).astype(jnp.float32)) / GATE_TAU
    qh = heads(q) * (GLA_DK ** -0.5)
    kh = heads(k)
    vh = heads(v)
    of, sf = _gla_scan(qh, kh, vh, heads(gf), s0f)

    def flip(a):
        return jnp.flip(a, axis=2)

    ob, sb = _gla_scan(flip(qh), flip(kh), flip(vh), flip(heads(gb)), s0b)
    o = (of + flip(ob)).transpose(0, 2, 1, 3).astype(h.dtype)
    o = _rmsnorm(o, gla_norm_g) * jax.nn.silu(r.reshape(bsz, t, GLA_HEADS, GLA_DV))
    o = o.reshape(bsz, t, MIX_GLA)

    u = ga * jax.nn.sigmoid(gg)
    if grid:
        rows = t // GRID_W
        u = _depthwise_conv(u.reshape(bsz * rows, GRID_W, MIX_CONV), conv_w, conv_b)
        u = u.reshape(bsz, t, MIX_CONV)
    else:
        u = _depthwise_conv(u, conv_w, conv_b)
    u = jax.nn.silu(_layernorm(u, conv_ln_g, conv_ln_b))

    out = jnp.einsum('btc,cd->btd', jnp.concatenate([o, u], axis=-1), w_out)
    return out, sf, sb

def _ec_moe(h, w_router, w_e_gate, w_e_up, w_e_down):
    bsz, t, _ = h.shape
    cap = EC_FACTOR * t // N_EXPERTS
    logits = jnp.einsum('btd,de->bte', h, w_router).astype(jnp.float32)
    aff = jax.nn.softmax(logits, axis=-1)
    gate, idx = lax.top_k(jnp.swapaxes(aff, 1, 2), cap)
    bidx = jnp.arange(bsz)[:, None, None]
    xs = h[bidx, idx]
    a = jnp.einsum('becd,edf->becf', xs, w_e_gate)
    u = jnp.einsum('becd,edf->becf', xs, w_e_up)
    y = jnp.einsum('becf,efd->becd', jax.nn.silu(a) * u, w_e_down)
    y = y * gate[..., None].astype(h.dtype)
    return jnp.zeros_like(h).at[bidx, idx].add(y)

def _layer(x, cond, grid, s0f, s0b, norm_mix_g, norm_ffn_g, w_mod, b_mod, w_in,
           w_decay_f, b_decay_f, w_decay_b, b_decay_b, gla_norm_g, conv_w, conv_b,
           conv_ln_g, conv_ln_b, w_out, w_router, w_e_gate, w_e_up, w_e_down):
    mod = (jax.nn.silu(cond) @ w_mod + b_mod)[:, None, :]
    sh1, sc1, gt1, sh2, sc2, gt2 = jnp.split(mod, 6, axis=-1)
    h = _rmsnorm(x, norm_mix_g) * (1.0 + sc1) + sh1
    mix, sf, sb = _mixer(h, grid, s0f, s0b, w_in, w_decay_f, b_decay_f, w_decay_b, b_decay_b,
                         gla_norm_g, conv_w, conv_b, conv_ln_g, conv_ln_b, w_out)
    x = x + gt1 * mix
    h = _rmsnorm(x, norm_ffn_g) * (1.0 + sc2) + sh2
    x = x + gt2 * _ec_moe(h, w_router, w_e_gate, w_e_up, w_e_down)
    return x, sf, sb

def setup_inputs(seed: int = 0) -> dict:
    key = jax.random.key(seed)
    ks = jax.random.split(key, 28)

    def nrm(k, shape, s):
        return jax.random.normal(k, shape, jnp.float32) * s

    st_shape = (DEC_BATCH, DEPTH, GLA_HEADS, GLA_DK, GLA_DV)
    return {
        'x_prompt': nrm(ks[0], (BATCH, SEQ, D_MODEL), 1.0),
        'x_sample': nrm(ks[1], (DEC_BATCH, DEC_SEQ, D_MODEL), 1.0),
        'state_gla_fwd': nrm(ks[2], st_shape, 1.0),
        'state_gla_bwd': nrm(ks[3], st_shape, 1.0),
        'c': nrm(ks[4], (DEC_BATCH, D_MODEL), 1.0),
        'c_ctx': nrm(ks[5], (D_MODEL,), 1.0),
        'norm_mix_g': 1.0 + nrm(ks[6], (DEPTH, D_MODEL), 0.05),
        'norm_ffn_g': 1.0 + nrm(ks[7], (DEPTH, D_MODEL), 0.05),
        'norm_final_g': 1.0 + nrm(ks[8], (D_MODEL,), 0.05),
        'w_mod': nrm(ks[9], (DEPTH, D_MODEL, 6 * D_MODEL), 0.5 * D_MODEL ** -0.5),
        'b_mod': nrm(ks[10], (DEPTH, 6 * D_MODEL), 0.01),
        'w_in': nrm(ks[11], (DEPTH, D_MODEL, IN_COLS), D_MODEL ** -0.5),
        'w_decay_f': nrm(ks[12], (DEPTH, GATE_RANK, GLA_KEY), GATE_RANK ** -0.5),
        'b_decay_f': nrm(ks[13], (DEPTH, GLA_KEY), 0.1),
        'w_decay_b': nrm(ks[14], (DEPTH, GATE_RANK, GLA_KEY), GATE_RANK ** -0.5),
        'b_decay_b': nrm(ks[15], (DEPTH, GLA_KEY), 0.1),
        'gla_norm_g': 1.0 + nrm(ks[16], (DEPTH, GLA_DV), 0.05),
        'conv_w': nrm(ks[17], (DEPTH, CONV_W, MIX_CONV), CONV_W ** -0.5),
        'conv_b': nrm(ks[18], (DEPTH, MIX_CONV), 0.01),
        'conv_ln_g': 1.0 + nrm(ks[19], (DEPTH, MIX_CONV), 0.05),
        'conv_ln_b': nrm(ks[20], (DEPTH, MIX_CONV), 0.01),
        'w_out': nrm(ks[21], (DEPTH, MIX_GLA + MIX_CONV, D_MODEL), (MIX_GLA + MIX_CONV) ** -0.5),
        'w_router': nrm(ks[22], (DEPTH, D_MODEL, N_EXPERTS), D_MODEL ** -0.5),
        'w_e_gate': nrm(ks[23], (DEPTH, N_EXPERTS, D_MODEL, D_EXPERT), D_MODEL ** -0.5),
        'w_e_up': nrm(ks[24], (DEPTH, N_EXPERTS, D_MODEL, D_EXPERT), D_MODEL ** -0.5),
        'w_e_down': nrm(ks[25], (DEPTH, N_EXPERTS, D_EXPERT, D_MODEL), D_EXPERT ** -0.5),
    }

def reference(x_prompt, x_sample, state_gla_fwd, state_gla_bwd, c, c_ctx,
              norm_mix_g, norm_ffn_g, norm_final_g, w_mod, b_mod, w_in,
              w_decay_f, b_decay_f, w_decay_b, b_decay_b, gla_norm_g,
              conv_w, conv_b, conv_ln_g, conv_ln_b, w_out, w_router,
              w_e_gate, w_e_up, w_e_down):
    xp = x_prompt
    xs = x_sample
    zero_state = jnp.zeros((x_prompt.shape[0], GLA_HEADS, GLA_DK, GLA_DV), jnp.float32)
    ctx_cond = c_ctx[None, :]
    fwd_states = []
    bwd_states = []
    for l in range(DEPTH):
        lw = (norm_mix_g[l], norm_ffn_g[l], w_mod[l], b_mod[l], w_in[l],
              w_decay_f[l], b_decay_f[l], w_decay_b[l], b_decay_b[l], gla_norm_g[l],
              conv_w[l], conv_b[l], conv_ln_g[l], conv_ln_b[l], w_out[l],
              w_router[l], w_e_gate[l], w_e_up[l], w_e_down[l])
        xp, sf, sb = _layer(xp, ctx_cond, False, zero_state, zero_state, *lw)
        fwd_states.append(sf)
        bwd_states.append(sb)
        xs, _, _ = _layer(xs, c, True,
                          state_gla_fwd[:, l].astype(jnp.float32),
                          state_gla_bwd[:, l].astype(jnp.float32), *lw)
    y_prompt = _rmsnorm(xp, norm_final_g)
    y_sample = _rmsnorm(xs, norm_final_g)
    new_state_gla_fwd = jnp.stack(fwd_states, axis=1).astype(x_prompt.dtype)
    new_state_gla_bwd = jnp.stack(bwd_states, axis=1).astype(x_prompt.dtype)
    return (y_prompt, y_sample, new_state_gla_fwd, new_state_gla_bwd)


_drawn_inputs = setup_inputs


def setup_inputs(seed=0):
    import zlib

    import numpy as np

    out = dict(_drawn_inputs(seed))
    spreads = {}
    factors = {'state_gla_fwd': 8.0,
     'state_gla_bwd': 8.0,
     'norm_ffn_g': 4.396,
     'gla_norm_g': 5.885,
     'conv_b': 8.0,
     'conv_ln_g': 6.408,
     'conv_ln_b': 8.0}
    for name, (base, spread) in spreads.items():
        noise = np.random.default_rng([zlib.crc32(name.encode()), seed]).standard_normal(out[name].shape)
        drawn = base * np.exp(spread * noise) if base else spread * noise
        out[name] = __import__('jax').numpy.asarray(drawn.astype(out[name].dtype))
    for name, factor in factors.items():
        out[name] = (out[name] * factor).astype(out[name].dtype)
    return out
```

```python
import concourse.bass as bass
from concourse import mybir
from contextlib import ExitStack

D = 1024
KC = D // 128
TP, TL = 256, 2048
NTOK = TP + TL
NTILE = NTOK // 128
BT = 512
NBLK = TL // BT
H, DK, DV, CH = 4, 64, 128, 64
RANK = 16
CW = 31
GRID = 64
NE, DE = 16, 1024
CAPP, CAPL = 2 * TP // NE, 2 * TL // NE
CAP = CAPL + CAPP
EPS = 1e-6
TAU = 16.0
OQ, OK, OV, OR, OZ, OGA, OGG = 0, 256, 512, 1024, 1536, 1568, 2080
PROJ_COLS = [OK, OQ, OGA, OGG, OGA + 256, OGG + 256, OV, OV + 256, OR, OR + 256]
NPROJ, NOUT, NEXP = len(PROJ_COLS), 4, 12
MOD1, MOD2 = 8, 16
RAW_PROJ_P = MOD1
RAW_MOD2 = RAW_PROJ_P + NPROJ
RAW_OUT_P = RAW_MOD2 + MOD2
RAW_PROJ_L = RAW_OUT_P + NOUT
RAW_OUT_L = RAW_PROJ_L + NPROJ * NBLK
SPL_PROJ_P = 0
SPL_OUT_P = SPL_PROJ_P + NPROJ
SPL_PROJ_L = SPL_OUT_P + NOUT
SPL_OUT_L = SPL_PROJ_L + NPROJ * NBLK
SPL_EXP = SPL_OUT_L + NOUT * NBLK


class Sig:

    def __init__(self, sem, p, l=None):
        self.sem, self.p, self.l = sem, p, p if l is None else l


def wait_alone(eng, settled, sem, value):
    eng.wait_ge(sem, value)
    eng.sem_inc(settled, 1)


class Blk:

    def __init__(self, i=None, settled=None):
        self.settled = settled
        self.prompt = i is None
        self.i = 0 if i is None else i
        self.T = TP if self.prompt else BT
        self.NT = self.T // 128
        self.NC = self.T // CH
        self.cond = 0 if self.prompt else 1

    def at(self, sig, j):
        return j if self.prompt else self.i * sig.l + (sig.p + j)

    def wait(self, eng, sig, j):
        v = self.at(sig, j)
        if isinstance(v, int) and v <= 0:
            return
        if self.settled is None:
            eng.wait_ge(sig.sem, v)
        else:
            wait_alone(eng, self.settled, sig.sem, v)


def hybrid_layer(nc, x_prompt, x_sample, state_gla_fwd, state_gla_bwd, c, c_ctx, norm_mix_g, norm_ffn_g,
                 norm_final_g, w_mod, b_mod, w_in, w_decay_f, b_decay_f, w_decay_b, b_decay_b, gla_norm_g,
                 conv_w, conv_b, conv_ln_g, conv_ln_b, w_out, w_router, w_e_gate, w_e_up, w_e_down,
                 y_prompt, y_sample, new_fwd, new_bwd):
    f32, f32r, bf16, u32 = mybir.dt.float32, mybir.dt.float32r, mybir.dt.bfloat16, mybir.dt.uint32
    ALU = mybir.AluOpType
    ACT = mybir.ActivationFunctionType
    AX = mybir.AxisListType
    ctx = ExitStack()
    with ctx:
        def sb(name, shape, dt=f32):
            return ctx.enter_context(nc.sbuf_tensor(name, shape, dt))

        def sem(name):
            return ctx.enter_context(nc.semaphore(name))

        def sig(name, p, l=None):
            return Sig(sem(name), p, l)

        def dram(name, shape):
            return nc.dram_tensor(name, shape, f32, kind="Internal").ap()

        x2_rows = dram("x2_rows", (NTOK, D))
        h2_rows = dram("h2_rows", (NTOK, D + NE))
        park_q = dram("park_q", (1 + NBLK, 128, H, BT))
        park_o = dram("park_o", (1 + NBLK, 128, H, BT))
        park_r = dram("park_r", (1 + NBLK, 128, H, BT))
        park_c = dram("park_c", (1 + NBLK, 128, H, BT))
        park_s = dram("park_s", (1 + NBLK, 128, BT // CH, H * DV))

        ident = sb("ident", [128, 128])
        ones = sb("ones", [128, 128])
        ones_b = sb("ones_b", [128, 128], bf16)
        before_b = sb("before_b", [128, 128], bf16)
        keep = sb("keep", [128, 2, 128], u32)
        reset = sb("reset", [128, H * BT], bf16)
        col = sb("col", [128, 112])
        scond = sb("scond", [128, 2, 8])
        wcv = sb("wcv", [128, 4, CW])
        mod = sb("mod", [128, 48, 2])
        A1 = sb("A1", [128, 8, 2])
        A2 = sb("A2", [128, 8, 2])
        wdec = sb("wdec", [2 * RANK, H * 128])
        wr = sb("wr", [128, KC, NE])
        wz_hl = sb("wz_hl", [128, 2, KC, 2 * RANK], f32r)
        eps = sb("eps", [128, 1])
        carry = sb("carry", [128, H * DV])
        dec = sb("dec", [128, 1 + NBLK, H, BT // CH])
        logits = sb("logits", [128, NTILE, NE])
        stat = sb("stat", [128, 32])
        raw = sb("raw", [128, 2, KC, 256])
        hl = sb("hl", [128, 2, 2, KC, 256], f32r)
        act_hl = sb("act_hl", [128, 2 * 2 * KC * CAP], f32r)
        WORK = 27400
        work = sb("work", [128, WORK])
        psum = [ctx.enter_context(nc.psum_tensor(f"bank{i}", [128, 512], f32)) for i in range(8)]

        h_hl = act_hl[:, 0:2 * KC * BT].rearrange("p (s k t) -> p s k t", s=2, k=KC)
        xe_hl = act_hl[:, 0:2 * KC * CAP].rearrange("p (s k t) -> p s k t", s=2, k=KC)
        he_hl = act_hl[:, 2 * KC * CAP:4 * KC * CAP].rearrange("p (s k t) -> p s k t", s=2, k=KC)

        def carve(sizes):
            out, at = {}, 0
            for name, n in sizes:
                out[name] = work[:, at:at + n]
                at += n
            assert at <= WORK, at
            return out

        W2 = carve([("x", 2 * D), ("xn", 2 * D), ("A", H * BT), ("B", H * BT), ("C", H * BT), ("q", H * BT),
                    ("k", H * BT), ("v", 4 * 512), ("kT", 512), ("pf", 512), ("pb", 512), ("pp", 512),
                    ("oi", 2 * 512), ("S", 9 * 512), ("acc", 4 * BT), ("r", 2 * BT), ("cl", H * BT // CH)])
        W2["u"], W2["z"] = W2["q"], W2["kT"]
        vecs, w_cv = W2["k"][0:112, 0:128], W2["k"][0:CW, 128:640]
        wz = W2["k"][:, 640:640 + KC * 2 * RANK].rearrange("p (k c) -> p k c", k=KC)
        x_t = W2["x"].rearrange("p (b d) -> p b d", b=2)
        xn_t = W2["xn"].rearrange("p (b d) -> p b d", b=2)
        v_t = W2["v"].rearrange("p (t c) -> p t c", t=4)
        oi_t = W2["oi"].rearrange("p (b h t) -> p b h t", b=2, h=H)
        S_t = W2["S"].rearrange("p (n c) -> p n c", n=9)
        W3 = carve([("q", H * BT), ("o", H * BT), ("r", H * BT), ("c", H * BT), ("S", 9 * 512), ("sq", 2 * BT),
                    ("rs", 2 * BT), ("y", KC * BT), ("x", 2 * D), ("xn", D), ("h2", KC * 128)])
        S3 = W3["S"].rearrange("p (n c) -> p n c", n=9)
        sq_t = W3["sq"].rearrange("p (b t) -> p b t", b=2)
        rs_t = W3["rs"].rearrange("p (b t) -> p b t", b=2)
        x3 = W3["x"].rearrange("p (b d) -> p b d", b=2)
        xn3 = W3["xn"]
        h2T = W3["h2"].rearrange("p (k t) -> p k t", k=KC)
        TE = NTILE * NE
        W4 = carve([("aff", TE), ("mx", NTILE), ("sm", NTILE), ("t1", TE), ("t2", TE), ("sel", TE), ("eq", TE),
                    ("pos", TE), ("tot", TE), ("inc", TE), ("rst", TE), ("cnt", 2 * NE), ("need", 2 * NE),
                    ("thr", 2 * NE), ("cand", 2 * NE), ("bit", 2 * NE), ("kp", 2 * NE), ("kk", 2 * NE),
                    ("idf", 3 * 2), ("iota", CAPL), ("mb", TE // 2), ("oh", 2 * CAPL // 2), ("idc", NTILE)])
        ids = sb("ids", [128, NE, 3], u32)
        W5 = carve([("raw2", 2 * KC * 256), ("xg", 3 * (D + NE)), ("h32", 2 * CAP), ("sg", 2 * CAP),
                    ("hx", 2 * CAP), ("yT", 4 * CAP), ("y", 3 * D), ("gate", 4)])
        xg = W5["xg"].rearrange("p (t d) -> p t d", t=3)
        h32e = W5["h32"].rearrange("p (b t) -> p b t", b=2)
        sg_t = W5["sg"].rearrange("p (b t) -> p b t", b=2)
        hx_t = W5["hx"].rearrange("p (b t) -> p b t", b=2)
        yT_t = W5["yT"].rearrange("p (b t) -> p b t", b=4)
        y_t = W5["y"].rearrange("p (t d) -> p t d", t=3)
        raw2 = W5["raw2"].rearrange("p (s k c) -> p s k c", s=2, k=KC)
        gate_t = W5["gate"]
        ids_g = sb("ids_g", [128, 3], u32)
        ids_s = sb("ids_s", [128, 3], u32)
        W6 = carve([("x", 4 * D), ("y", 4 * D), ("g", D), ("junk", D)])
        x6 = W6["x"].rearrange("p (b d) -> p b d", b=4)
        y6 = W6["y"].rearrange("p (b d) -> p b d", b=4)

        V_C, V_CTX, V_GM, V_GF, V_BM, V_CB, V_LG, V_LB, V_GN, V_BD = 0, 8, 16, 24, 32, 80, 84, 88, 92, 93
        NV = 97

        s_alone = sem("s_alone")
        s_vec = sem("s_vec")
        s_cst = sem("s_cst")
        s_vconst = sem("s_vconst")
        s_vT, s_col = sem("s_vT"), sem("s_col")
        s_silc = sem("s_silc")
        s_wz = sem("s_wz")
        s_mod, s_modv = sem("s_mod"), sem("s_modv")
        s_raw = [sem("s_raw0"), sem("s_raw1")]
        s_rawfree = [sem("s_rawfree0"), sem("s_rawfree1")]
        s_hi = sem("s_hi")
        s_lo = [sem("s_lo0"), sem("s_lo1")]
        s_unit = sem("s_unit")
        s_ph = sem("s_ph")
        s_xin = [sig("s_xin0", 16, 32), sig("s_xin1", 16, 32)]
        s_sq, s_rt, s_rstd, s_xn = sig("s_sq", 2, 4), sig("s_rt", 2, 4), sig("s_rstd", 2, 4), sig("s_xn", 2, 4)
        s_xT, s_h32, s_hhi, s_hlo = sig("s_xT", 2, 4), sig("s_h32", 2, 4), sig("s_hhi", 2, 4), sig("s_hlo", 2, 4)
        s_z, s_zt = sig("s_z", 1), sig("s_zt", 1)
        s_dec, s_abs, s_min = sig("s_dec", 4), sig("s_abs", 4), sig("s_min", 4)
        s_ln = sig("s_ln", 2)
        s_g, s_cum = sig("s_g", 1), sig("s_cum", 2)
        s_cl = sig("s_cl", 3)
        s_D = sig("s_D", 1)
        s_ex = sig("s_ex", 3)
        s_kfb, s_qfb = sig("s_kfb", 1), sig("s_qfb", 1)
        s_dk = sig("s_dk", 3)
        s_sg, s_u, s_conv = sig("s_sg", 4), sig("s_u", 4), sig("s_conv", 4 * CW)
        s_v, s_r = sig("s_v", 2), sig("s_r", 4)
        s_kt, s_kte = sig("s_kt", 2, 4), sig("s_kte", 2, 4)
        s_sf, s_sb = sig("s_sf", 2, 4), sig("s_sb", 2, 4)
        s_pf, s_pb, s_pp = sig("s_pf", 2, 4), sig("s_pb", 2, 4), sig("s_pp", 2, 4)
        s_upd, s_ue, s_fs = sig("s_upd", 4, 8), sig("s_ue", 4, 8), sig("s_fs", 4, 8)
        s_c0, s_c1 = sig("s_c0", 1), sig("s_c1", 1)
        s_oi, s_oe = sig("s_oi", 2, 4), sig("s_oe", 2, 4)
        s_qst, s_sst, s_cstr = sig("s_qst", 16), sig("s_sst", 16), sig("s_cstr", 16)
        s_ost = [sig("s_ost0", 16, 32), sig("s_ost1", 16, 32)]
        s_rst = [sig("s_rst0", 32), sig("s_rst1", 32)]
        s_st = sem("s_st")
        t_q, t_o, t_r, t_c, t_S = sig("t_q", 16), sig("t_o", 16), sig("t_r", 16), sig("t_c", 16), sig("t_S", 32)
        t_x = [sig("t_x0", 16, 32), sig("t_x1", 16, 32)]
        t_c0, t_bs, t_c1 = sig("t_c0", 1), sig("t_bs", 4, 8), sig("t_c1", 1)
        t_in, t_o1, t_sq, t_ms, t_rt, t_rc, t_on, t_og, t_hi, t_lo = (
            sig("t_in", 4), sig("t_o1", 4), sig("t_sq", 4), sig("t_ms", 4), sig("t_rt", 4), sig("t_rc", 4),
            sig("t_on", 4), sig("t_og", 4), sig("t_hi", 8), sig("t_lo", 8))
        t_me, t_xc, t_csq, t_va, t_crt, t_crc, t_cn, t_si = (
            sig("t_me", 1), sig("t_xc", 4), sig("t_csq", 4), sig("t_va", 1), sig("t_crt", 1), sig("t_crc", 1),
            sig("t_cn", 4), sig("t_si", 4))
        t_cs = sig("t_cs", 4)
        t_y = sig("t_y", 4)
        t_yT, t_x2, t_s2, t_r2, t_i2, t_xn, t_xT, t_h2, t_ro, t_lg = (
            sig("t_yT", 2, 4), sig("t_x2", 2, 4), sig("t_s2", 2, 4), sig("t_r2", 2, 4), sig("t_i2", 2, 4),
            sig("t_xn", 2, 4), sig("t_xT", 2, 4), sig("t_h2", 2, 4), sig("t_ro", 2, 4), sig("t_lg", 2, 4))
        t_x2st = [sig("t_x2st0", 16, 32), sig("t_x2st1", 16, 32)]
        t_h2st = sig("t_h2st", 32, 64)
        k_v = sem("k_v")
        k_e = sem("k_e")
        k_m, k_cnt = sem("k_m"), sem("k_cnt")
        k_p = sem("k_p")
        k_oh, k_id, k_ev = sem("k_oh"), sem("k_id"), sem("k_ev")
        k_af = sem("k_af")
        e_raw = [sem(f"e_raw{i}") for i in range(4)]
        e_ids, e_gat, e_gate = sem("e_ids"), sem("e_gat"), sem("e_gate")
        e_xk, e_xh, e_xhi, e_xlo = sem("e_xk"), sem("e_xh"), sem("e_xhi"), sem("e_xlo")
        e_si, e_h, e_hhi, e_hlo = sem("e_si"), sem("e_h"), sem("e_hhi"), sem("e_hlo")
        e_yT, e_yt, e_yev, e_sc = sem("e_yT"), sem("e_yt"), sem("e_yev"), sem("e_sc")
        f_g, f_x, f_sq, f_rt, f_rc, f_y, f_st = (sem("f_g"), [sem(f"f_x{i}") for i in range(4)], sem("f_sq"),
                                                 sem("f_rt"), sem("f_rc"), sem("f_y"),
                                                 [sem(f"f_st{i}") for i in range(4)])

        def stage_end(eng, n, group):
            eng.drain().then_inc(s_ph, 1)
            eng.wait_ge(s_ph, 5 * n)

        block = ctx.enter_context(nc.Block())

        w_in_v = w_in[0].rearrange("(k p) c -> p k c", p=128)
        w_out_v = w_out[0].rearrange("(k p) c -> p k c", p=128)
        w_mod_v = w_mod[0].rearrange("(k p) c -> p k c", p=128)

        def slot(base, j):
            return (base + j) % 2

        def turn(base, per, i, j):
            return (base + j) // 2 + (per // 2) * i if not isinstance(i, int) or i else (base + j) // 2

        def wait_pos(eng, s, v):
            if isinstance(v, int) and v <= 0:
                return
            eng.wait_ge(s, v)

        @block.sync
        def _(sp):
            def load_unit(base, per, i, j, src):
                s = slot(base, j)
                v = turn(base, per, i, j)
                if not isinstance(v, int) or v > 0:
                    wait_alone(sp, s_alone, s_rawfree[s], v)
                sp.dma_start(raw[:, s], src).then_inc(s_raw[s], 16)

            for r, n, a in ((V_C, 8, c[0]), (V_CTX, 8, c_ctx), (V_GM, 8, norm_mix_g[0]), (V_GF, 8, norm_ffn_g[0]),
                            (V_BM, 48, b_mod[0]), (V_CB, 4, conv_b[0]), (V_LG, 4, conv_ln_g[0]),
                            (V_LB, 4, conv_ln_b[0]), (V_GN, 1, gla_norm_g[0])):
                sp.dma_start(vecs[r:r + n, :], a.rearrange("(a b) -> a b", b=128)).then_inc(s_vec, 16)
            for a, o in ((b_decay_f, 0), (b_decay_b, 64)):
                sp.dma_start(vecs[V_BD:V_BD + 4, o:o + 64], a[0].rearrange("(h k) -> h k", h=H)).then_inc(s_vec, 16)
            sp.dma_start(w_cv[:, :], conv_w[0]).then_inc(s_vec, 16)
            sp.dma_start(wr[:, :, :], w_router[0].rearrange("(k p) e -> p k e", p=128)).then_inc(s_vec, 16)
            sp.dma_start(wz[:, :, :], w_in_v[:, :, OZ:OZ + 2 * RANK]).then_inc(s_vec, 16)
            sp.wait_ge(s_cst, 4)
            for a, r, o in ((w_decay_f, 0, 0), (w_decay_b, RANK, 64)):
                sp.dma_start(wdec[r:r + RANK, :].rearrange("r (h c) -> r h c", h=H)[:, :, o:o + 64],
                             a[0].rearrange("r (h k) -> r h k", h=H)).then_inc(s_vec, 16)
            for j in range(MOD1):
                load_unit(0, MOD1, 0, j, w_mod_v[:, :, 256 * j:256 * j + 256])

            def stage2(b):
                n = 0 if b.prompt else b.i + 1
                x_src = x_prompt[0] if b.prompt else x_sample[0].rearrange("(n t) d -> n t d", t=BT)[b.i]
                base, per = (RAW_PROJ_P, NPROJ) if b.prompt else (RAW_PROJ_L, NPROJ)
                for t in range(b.NT):
                    if t == 2:
                        for j in range(2):
                            load_unit(base, per, b.i, j, w_in_v[:, :, PROJ_COLS[j]:PROJ_COLS[j] + 256])
                    b.wait(sp, s_xn, t - 1)
                    sp.dma_start(x_t[:, t % 2, :], x_src[128 * t:128 * t + 128, :]).then_inc(s_xin[t % 2].sem, 16)
                for j in range(0 if b.NT == 2 else 2, NPROJ):
                    load_unit(base, per, b.i, j, w_in_v[:, :, PROJ_COLS[j]:PROJ_COLS[j] + 256])
                    if j == 4:
                        b.wait(sp, s_dk, 3)
                        sp.dma_start(park_q[n, :, :, 0:b.T],
                                     W2["B"][:, 0:H * b.T].rearrange("p (h t) -> p h t", h=H)).then_inc(s_qst.sem, 16)
                for rt in range(4):
                    b.wait(sp, s_r, rt + 1)
                    sp.dma_start(park_r[n, :, rt, 0:b.T], W2["r"][:, (rt % 2) * BT:(rt % 2) * BT + b.T])\
                      .then_inc(s_rst[rt % 2].sem, 16)

            def stage2_parks(q, b):
                n = 0 if b.prompt else b.i + 1
                for t in range(b.NT):
                    b.wait(q, s_oe, t + 1)
                    q.dma_start(park_o[n, :, :, 128 * t:128 * t + 128], oi_t[:, t % 2]).then_inc(s_ost[t % 2].sem, 16)
                b.wait(q, s_fs, b.NC)
                b.wait(q, s_ue, b.NC)
                q.dma_start(park_s[n, :, 0:b.NC, :], S_t[:, 0:b.NC, :]).then_inc(s_sst.sem, 16)
                b.wait(q, s_conv, 4 * CW)
                q.dma_start(park_c[n, :, :, 0:b.T],
                            W2["acc"][:, 0:4 * b.T].rearrange("p (h t) -> p h t", h=4)).then_inc(s_cstr.sem, 16)

            def stage2_done(q, b):
                for s in (s_qst, s_sst, s_cstr, *s_ost, *s_rst):
                    q.wait_ge(s.sem, b.at(s, s.p if b.prompt else s.l))

            def stage3_loads(b):
                n = 0 if b.prompt else NBLK - b.i
                for src, name, sg_, use, cnt in ((park_q, "q", t_q, t_in, 0), (park_o, "o", t_o, t_lo, 0),
                                                 (park_r, "r", t_r, t_og, 0), (park_c, "c", t_c, t_lo, 0)):
                    b.wait(sp, use, cnt)
                    sp.dma_start(W3[name][:, 0:H * b.T].rearrange("p (h t) -> p h t", h=H),
                                 src[n, :, :, 0:b.T]).then_inc(sg_.sem, 16)
                    if name == "q":
                        b.wait(sp, t_c1, 0)
                        sp.dma_start(S3[0:64, 1:b.NC + 1, :], park_s[n, 0:64, 0:b.NC, :]).then_inc(t_S.sem, 16)
                        sp.dma_start(S3[64:128, 0:b.NC, :], park_s[n, 64:128, 0:b.NC, :]).then_inc(t_S.sem, 16)

            def stage3(b):
                base = RAW_OUT_P if b.prompt else RAW_OUT_L
                for j in range(NOUT):
                    load_unit(base, NOUT, b.i, j, w_out_v[:, :, 256 * j:256 * j + 256])
                x_src = x_prompt[0] if b.prompt else x_sample[0].rearrange("(n t) d -> n t d", t=BT)[NBLK - 1 - b.i]
                row = x2_rows[0:TP] if b.prompt else \
                    x2_rows[TP:NTOK].rearrange("(n t) d -> n t d", t=BT)[NBLK - 1 - b.i]
                hrow = h2_rows[0:TP] if b.prompt else \
                    h2_rows[TP:NTOK].rearrange("(n t) d -> n t d", t=BT)[NBLK - 1 - b.i]

                def load_x(t):
                    if t >= 2:
                        b.wait(sp, t_x2st[t % 2], 16 * (t // 2))
                        b.wait(sp, t_xn, t - 1)
                    else:
                        b.wait(sp, t_x2st[t % 2], 0)
                        b.wait(sp, t_xn, 0)
                    sp.dma_start(x3[:, t % 2, :], x_src[128 * t:128 * t + 128, :]).then_inc(t_x[t % 2].sem, 16)

                load_x(0)
                load_x(1)
                for t in range(b.NT):
                    b.wait(sp, t_x2, t + 1)
                    sp.dma_start(row[128 * t:128 * t + 128, :], x3[:, t % 2, :]).then_inc(t_x2st[t % 2].sem, 16)
                    b.wait(sp, t_xn, t + 1)
                    sp.dma_start(hrow[128 * t:128 * t + 128, 0:D], xn3[:, :]).then_inc(t_h2st.sem, 16)
                    if t + 2 < b.NT:
                        load_x(t + 2)

            def stage3_done(b):
                for s in t_x2st:
                    sp.wait_ge(s.sem, b.at(s, s.p if b.prompt else s.l))

            p = Blk()
            stage2(p)
            stage2_parks(sp, p)
            for j in range(MOD2):
                load_unit(RAW_MOD2, MOD2, 0, j, w_mod_v[:, :, 256 * (MOD1 + j):256 * (MOD1 + j) + 256])
            stage2_done(sp, p)
            p.wait(sp, s_c1, 1)
            sp.dma_start(new_fwd[0, 0].rearrange("h k v -> k h v"),
                         carry[0:64, :].rearrange("k (h v) -> k h v", h=H)).then_inc(s_st, 16)
            stage_end(sp, 1, 0)
            stage3_loads(p)
            stage3(p)
            stage3_done(p)
            p.wait(sp, t_c1, 1)
            sp.dma_start(new_bwd[0, 0].rearrange("h k v -> k h v"),
                         carry[64:128, :].rearrange("k (h v) -> k h v", h=H)).then_inc(s_st, 16)
            sp.wait_ge(s_st, 32)
            sp.dma_start(carry[0:64, :].rearrange("k (h v) -> k h v", h=H),
                         state_gla_fwd[0, 0].rearrange("h k v -> k h v")).then_inc(s_st, 16)
            sp.dma_start(carry[64:128, :].rearrange("k (h v) -> k h v", h=H),
                         state_gla_bwd[0, 0].rearrange("h k v -> k h v")).then_inc(s_st, 16)
            stage_end(sp, 2, 0)
            with sp.Fori(0, NBLK) as i:
                b = Blk(i, s_alone)
                stage2(b)
                stage2_parks(sp, b)
            sp_last = Blk(NBLK - 1)
            stage2_done(sp, sp_last)
            stage_end(sp, 3, 0)
            with sp.Fori(0, NBLK) as i:
                b = Blk(i, s_alone)
                stage3_loads(b)
                stage3(b)
            stage3_done(sp_last)
            stage_end(sp, 4, 0)
            sp.wait_ge(k_v, 5)
            sp.dma_start(h2_rows[:, D:D + NE].rearrange("(t p) e -> p t e", p=128),
                         W4["aff"].rearrange("p (t e) -> p t e", e=NE)).then_inc(k_af, 16)
            sp.wait_ge(k_af, 16)
            stage_end(sp, 5, 0)

            def expert_units(e):
                for j in range(NEXP):
                    s = j % 4
                    if j < 8:
                        src = (w_e_gate if j % 2 == 0 else w_e_up)[0, e]
                        o = 256 * (j // 2)
                    else:
                        src, o = w_e_down[0, e], 256 * (j - 8)
                    wait_alone(sp, s_alone, s_lo[j % 2], 2 * ((SPL_EXP + j - 4) // 2 + 1) + NEXP * e)
                    dst = raw[:, s] if s < 2 else raw2[:, s - 2]
                    sp.dma_start(dst, src.rearrange("(k p) c -> p k c", p=128)[:, :, o:o + 256]).then_inc(e_raw[s], 16)

            with sp.Fori(0, NE) as e:
                expert_units(e)
            stage_end(sp, 6, 0)
            sp.dma_start(W6["g"], norm_final_g.partition_broadcast(128)).then_inc(f_g, 16)
            for t in range(NTILE + 2):
                if t < NTILE:
                    if t >= 4:
                        sp.wait_ge(f_y, t - 3)
                    sp.dma_start(x6[:, t % 4, :], x2_rows[128 * t:128 * t + 128, :]).then_inc(f_x[t % 4], 16)
                if t >= 2:
                    u = t - 2
                    sp.wait_ge(f_y, u + 1)
                    dst = y_prompt[0, 128 * u:128 * u + 128, :] if u < TP // 128 else \
                        y_sample[0, 128 * u - TP:128 * u - TP + 128, :]
                    sp.dma_start(dst, y6[:, u % 4, :]).then_inc(f_st[u % 4], 16)
            for q in range(4):
                sp.wait_ge(f_st[q], 16 * len(range(q, NTILE, 4)))

        @block.scalar
        def _(act):
            def hi_halves(base, per, i, j):
                n = base + j
                rb = {SPL_PROJ_P: RAW_PROJ_P, SPL_OUT_P: RAW_OUT_P, SPL_PROJ_L: RAW_PROJ_L, SPL_OUT_L: RAW_OUT_L}[base]
                s = slot(rb, j)
                assert s == n % 2
                act.wait_ge(s_raw[s], 16 * (turn(rb, per, i, j) + 1))
                wait_pos(act, s_unit, per * i + (n - 1) if not isinstance(i, int) or i else n - 1)
                for q in range(2):
                    act.activation(hl[:, s, 0, :, 128 * q:128 * q + 128], raw[:, s, :, 128 * q:128 * q + 128],
                                   ACT.Copy).then_inc(s_hi, 1)

            act.wait_ge(s_cst, 23)
            act.wait_ge(s_col, 1)
            act.activation(scond[:, 0, :], col[:, V_CTX:V_CTX + 8], ACT.Silu)
            act.activation(scond[:, 1, :], col[:, V_C:V_C + 8], ACT.Silu).then_inc(s_silc, 1)
            act.wait_ge(s_vec, 16 * 16)
            act.activation(wz_hl[:, 0], wz[:, :, :], ACT.Copy).then_inc(s_wz, 1)

            def unit_done(b, base, per, j):
                act.wait_ge(s_unit, per * b.i + (base + j + 1) if not b.prompt else base + j + 1)

            def stage2(b):
                base = SPL_PROJ_P if b.prompt else SPL_PROJ_L
                n = 0 if b.prompt else b.i + 1
                T = b.T
                hi_halves(base, NPROJ, b.i, 0)
                hi_halves(base, NPROJ, b.i, 1)
                for t in range(b.NT):
                    b.wait(act, s_xin[t % 2], 16 * (t // 2 + 1))
                    b.wait(act, s_hlo, t - 1)
                    act.activation(xn_t[:, t % 2, :], x_t[:, t % 2, :], ACT.Square,
                                   accum_out=stat[:, t:t + 1]).then_inc(s_sq.sem, 1)
                    b.wait(act, s_sq, t + 1)
                    act.activation(stat[:, 4 + t:5 + t], stat[:, t:t + 1], ACT.Sqrt, bias=eps[:, :], scale=1.0 / D)\
                       .then_inc(s_rt.sem, 1)
                    b.wait(act, s_rstd, t + 1)
                    act.activation(xn_t[:, t % 2, :], x_t[:, t % 2, :], ACT.Copy, scale=stat[:, 8 + t:9 + t])\
                       .then_inc(s_xn.sem, 1)
                    if t >= 1:
                        hi_tile(b, t - 1)
                hi_tile(b, b.NT - 1)
                b.wait(act, s_upd, 0)
                b.wait(act, s_z, 1)
                act.activation(W2["z"][0:2 * RANK, 0:T], psum[4][0:2 * RANK, 0:T], ACT.Copy).then_inc(s_zt.sem, 1)
                copies(b, base, 0, "k", 1.0, s_kfb, s_dk)
                hi_halves(base, NPROJ, b.i, 2)
                b.wait(act, s_qst, 0)
                for h in range(H):
                    b.wait(act, s_min, h + 1)
                    act.activation(W2["B"][:, h * T:(h + 1) * T], psum[4 + h][:, 0:T], ACT.Abs,
                                   bias=col[:, V_BD + h:V_BD + h + 1]).then_inc(s_abs.sem, 1)
                b.wait(act, s_abs, 4)
                act.activation(W2["B"][:, 0:H * T], W2["B"][:, 0:H * T], ACT.Exp, scale=-1.0).then_inc(s_ln.sem, 1)
                b.wait(act, s_ln, 1)
                act.activation(W2["B"][:, 0:H * T], W2["B"][:, 0:H * T], ACT.Ln, bias=1.0).then_inc(s_ln.sem, 1)
                copies(b, base, 1, "q", DK ** -0.5, s_qfb, s_dk)
                hi_halves(base, NPROJ, b.i, 3)
                b.wait(act, s_cum, 2)
                b.wait(act, s_g, 1)
                act.activation(W2["B"][:, 0:H * T], W2["C"][:, 0:H * T], ACT.Exp, scale=1.0 / TAU).then_inc(s_ex.sem, 1)
                b.wait(act, s_cl, 2)
                act.activation(dec[:, n, :, 0:b.NC], W2["cl"][:, 0:H * b.NC].rearrange("p (h c) -> p h c", h=H),
                               ACT.Exp, scale=1.0 / TAU).then_inc(s_D.sem, 1)
                b.wait(act, s_cl, 3)
                act.activation(W2["A"][:, 0:H * T], W2["A"][:, 0:H * T], ACT.Exp, scale=1.0 / TAU).then_inc(s_ex.sem, 1)
                act.activation(W2["C"][:, 0:H * T], W2["C"][:, 0:H * T], ACT.Exp, scale=-1.0 / TAU)\
                   .then_inc(s_ex.sem, 1)
                unit_done(b, base, NPROJ, 2)
                hi_halves(base, NPROJ, b.i, 4)
                sigmoids(b, base, 3, 0)
                hi_halves(base, NPROJ, b.i, 5)
                unit_done(b, base, NPROJ, 4)
                hi_halves(base, NPROJ, b.i, 6)
                sigmoids(b, base, 5, 2)
                hi_halves(base, NPROJ, b.i, 7)
                values(b, base, 6)
                hi_halves(base, NPROJ, b.i, 8)
                values(b, base, 7)
                hi_halves(base, NPROJ, b.i, 9)
                gla(b, 0)
                gates(b, base, 8, 0)
                gla(b, 1)
                gates(b, base, 9, 2)
                for t in range(2, b.NT):
                    gla(b, t)

            def hi_tile(b, t):
                b.wait(act, s_h32, t + 1)
                act.activation(h_hl[:, 0, :, 128 * t:128 * t + 128],
                               xn_t[:, t % 2, :].rearrange("p (k t) -> p k t", k=KC), ACT.Copy).then_inc(s_hhi.sem, 1)

            def copies(b, base, j, name, scale, done, used):
                unit_done(b, base, NPROJ, j)
                b.wait(act, used, 0)
                if name == "q":
                    b.wait(act, s_conv, 0)
                for h in range(H):
                    for q in range(2):
                        last = act.activation(W2[name][64 * q:64 * q + 64, h * b.T:(h + 1) * b.T],
                                              psum[2 * (j % 2) + h // 2][64 * (h % 2):64 * (h % 2) + 64, 0:b.T],
                                              ACT.Copy, scale=scale)
                last.then_inc(done.sem, 1)

            def sigmoids(b, base, j, ct):
                unit_done(b, base, NPROJ, j)
                for q in range(2):
                    b.wait(act, s_dk, 3)
                    act.activation(W2["u"][:, (ct + q) * BT:(ct + q) * BT + b.T], psum[2 * (j % 2) + q][:, 0:b.T],
                                   ACT.Sigmoid).then_inc(s_sg.sem, 1)

            def values(b, base, j):
                unit_done(b, base, NPROJ, j)
                b.wait(act, s_oi, 0)
                for q in range(b.NT // 2):
                    last = act.activation(v_t[:, 2 * q:2 * q + 2, 256 * (j - 6):256 * (j - 6) + 256],
                                          psum[2 * (j % 2) + q][:, :].rearrange("p (t c) -> p t c", t=2), ACT.Copy)
                last.then_inc(s_v.sem, 1)

            def gates(b, base, j, rt):
                unit_done(b, base, NPROJ, j)
                for q in range(2):
                    b.wait(act, s_rst[(rt + q) % 2], 16 * ((rt + q) // 2))
                    act.activation(W2["r"][:, ((rt + q) % 2) * BT:((rt + q) % 2) * BT + b.T],
                                   psum[2 * (j % 2) + q][:, 0:b.T], ACT.Silu).then_inc(s_r.sem, 1)

            def gla(b, t):
                b.wait(act, s_kt, t + 1)
                b.wait(act, s_upd, 2 * t)
                act.activation(W2["kT"][:, :], psum[4][:, :], ACT.Copy).then_inc(s_kte.sem, 1)
                if t == 0:
                    b.wait(act, s_sst, 0)
                    b.wait(act, s_c1, 0)
                for q in range(2):
                    cc = 2 * t + q
                    b.wait(act, s_upd, cc + 1)
                    act.activation(S_t[64:128, cc, :], psum[4 + q][64:128, :], ACT.Copy)
                    act.activation(S_t[0:64, cc + 1, :], psum[4 + q][0:64, :], ACT.Copy).then_inc(s_ue.sem, 1)
                b.wait(act, s_oi, t + 1)
                b.wait(act, s_ost[t % 2], 16 * (t // 2))
                act.activation(oi_t[:, t % 2], psum[7][:, :].rearrange("p (h t) -> p h t", h=H), ACT.Copy)\
                   .then_inc(s_oe.sem, 1)

            def stage3(b):
                base = SPL_OUT_P if b.prompt else SPL_OUT_L
                T = b.T
                hi_halves(base, NOUT, b.i, 0)
                hi_halves(base, NOUT, b.i, 1)
                for h in range(H):
                    b.wait(act, t_o1, h + 1)
                    b.wait(act, t_ms, h - 1)
                    if h < 2:
                        b.wait(act, t_va, 0)
                    act.activation(sq_t[:, h % 2, 0:T], W3["o"][:, h * T:(h + 1) * T], ACT.Square).then_inc(t_sq.sem, 1)
                for h in range(H):
                    b.wait(act, t_ms, h + 1)
                    b.wait(act, t_on, h - 1)
                    if h < 2:
                        b.wait(act, t_cn, 0)
                    act.activation(rs_t[:, h % 2, 0:T], psum[4 + h][:, 0:T], ACT.Sqrt, bias=eps[:, :], scale=1.0 / DV)\
                       .then_inc(t_rt.sem, 1)
                    if h >= 1:
                        cat_hi(b, h - 1, "o", t_og, h)
                cat_hi(b, H - 1, "o", t_og, H)
                for ct in range(4):
                    b.wait(act, t_xc, ct + 1)
                    b.wait(act, t_ms, 4)
                    if ct >= 2:
                        b.wait(act, t_csq, ct - 1)
                        b.wait(act, t_cs, ct - 1)
                    act.activation(sq_t[:, ct % 2, 0:T], W3["c"][:, ct * T:(ct + 1) * T], ACT.Square)\
                       .then_inc(t_csq.sem, 1)
                b.wait(act, t_va, 1)
                b.wait(act, t_on, 4)
                act.activation(rs_t[:, 0, 0:T], psum[1][:, 0:T], ACT.Sqrt, bias=eps[:, :], scale=1.0 / 512)\
                   .then_inc(t_crt.sem, 1)
                for ct in range(4):
                    b.wait(act, t_cn, ct + 1)
                    act.activation(W3["c"][:, ct * T:(ct + 1) * T], W3["c"][:, ct * T:(ct + 1) * T], ACT.Silu,
                                   scale=col[:, V_LG + ct:V_LG + ct + 1],
                                   bias=col[:, V_LB + ct:V_LB + ct + 1]).then_inc(t_si.sem, 1)
                    if ct >= 1:
                        cat_hi(b, 4 + ct - 1, "c", t_si, ct)
                cat_hi(b, 7, "c", t_si, 4)
                for j in range(NOUT):
                    act.wait_ge(s_unit, NOUT * b.i + (base + j + 1) if not b.prompt else base + j + 1)
                    for q in range(2):
                        d = 2 * j + q
                        last = act.activation(W3["y"][:, d * T:(d + 1) * T], psum[2 * (j % 2) + q][:, 0:T], ACT.Copy,
                                              scale=mod[:, 16 + d, b.cond:b.cond + 1])
                    last.then_inc(t_y.sem, 1)
                    if j + 2 < NOUT:
                        hi_halves(base, NOUT, b.i, j + 2)
                for t in range(b.NT):
                    b.wait(act, t_x2, t + 1)
                    b.wait(act, t_h2st, 16 * t)
                    b.wait(act, t_xT, t)
                    act.activation(xn3[:, :], x3[:, t % 2, :], ACT.Square, accum_out=stat[:, t:t + 1])\
                       .then_inc(t_s2.sem, 1)
                    b.wait(act, t_s2, t + 1)
                    act.activation(stat[:, 4 + t:5 + t], stat[:, t:t + 1], ACT.Sqrt, bias=eps[:, :], scale=1.0 / D)\
                       .then_inc(t_r2.sem, 1)
                    b.wait(act, t_i2, t + 1)
                    act.activation(xn3[:, :], x3[:, t % 2, :], ACT.Copy, scale=stat[:, 8 + t:9 + t])\
                       .then_inc(t_xn.sem, 1)

            def cat_hi(b, k, name, s, j):
                b.wait(act, s, j)
                o = (k % 4) * b.T
                act.activation(h_hl[:, 0, k, 0:b.T], W3[name][:, o:o + b.T], ACT.Copy).then_inc(t_hi.sem, 1)

            p = Blk()
            stage2(p)
            stage_end(act, 1, 1)
            stage3(p)
            stage_end(act, 2, 1)
            with act.Fori(0, NBLK) as i:
                stage2(Blk(i))
            stage_end(act, 3, 1)
            with act.Fori(0, NBLK) as i:
                stage3(Blk(i))
            stage_end(act, 4, 1)
            act.wait_ge(k_v, 2)
            act.activation(W4["aff"], W4["aff"], ACT.Exp).then_inc(k_e, 1)
            stage_end(act, 5, 1)

            def ehi(e, j):
                s = j % 4
                act.wait_ge(e_raw[s], 48 * e + 16 * (j // 4 + 1))
                act.wait_ge(s_unit, NEXP * e + (SPL_EXP + j - 1))
                src = raw[:, s] if s < 2 else raw2[:, s - 2]
                for q in range(2):
                    act.activation(hl[:, j % 2, 0, :, 128 * q:128 * q + 128], src[:, :, 128 * q:128 * q + 128],
                                   ACT.Copy).then_inc(s_hi, 1)

            def xe_hi(e, k):
                act.wait_ge(e_xh, 8 * e + (k + 1))
                act.activation(xe_hl[:, 0, k, :], h32e[:, k % 2, :], ACT.Copy).then_inc(e_xhi, 1)

            def expert(e, last):
                for j in range(NEXP):
                    if j + 2 < NEXP or not last:
                        ehi(e, j + 2)
                    act.wait_ge(s_unit, NEXP * e + (SPL_EXP + j + 1))
                    for q in range(2):
                        if j < 8 and j % 2 == 0:
                            ft = j + q
                            wait_pos(act, e_h, 8 * e + max(ft - 1, 0))
                            act.activation(sg_t[:, ft % 2, :], psum[q][:, 0:CAP], ACT.Silu).then_inc(e_si, 1)
                        elif j < 8:
                            ft = j - 1 + q
                            act.wait_ge(e_h, 8 * e + (ft + 1))
                            act.activation(he_hl[:, 0, ft, :], hx_t[:, ft % 2, :], ACT.Copy).then_inc(e_hhi, 1)
                        else:
                            d = 2 * (j - 8) + q
                            wait_pos(act, e_yt, 8 * e + max(d - 3, 0))
                            act.activation(yT_t[:, d % 4, 0:CAPL], psum[2 * (j % 2) + q][:, 0:CAPL], ACT.Copy,
                                           scale=mod[:, 40 + d, 1:2])
                            act.activation(yT_t[:, d % 4, CAPL:CAP], psum[2 * (j % 2) + q][:, CAPL:CAP], ACT.Copy,
                                           scale=mod[:, 40 + d, 0:1]).then_inc(e_yT, 1)
                    if j >= 8 and not last:
                        xe_hi(e + 1, 2 * (j - 8))
                        xe_hi(e + 1, 2 * (j - 8) + 1)

            for k in range(KC):
                xe_hi(0, k)
            ehi(0, 0)
            ehi(0, 1)
            with act.Fori(0, NE - 1) as e:
                expert(e, False)
            expert(NE - 1, True)
            stage_end(act, 6, 1)
            for t in range(NTILE):
                act.wait_ge(f_x[t % 4], 16 * (t // 4 + 1))
                act.activation(W6["junk"], x6[:, t % 4, :], ACT.Square, accum_out=stat[:, t % 8:t % 8 + 1])\
                   .then_inc(f_sq, 1)
                act.wait_ge(f_sq, t + 1)
                if t >= 8:
                    act.wait_ge(f_rc, t - 7)
                act.activation(stat[:, 8 + t % 8:9 + t % 8], stat[:, t % 8:t % 8 + 1], ACT.Sqrt, bias=eps[:, :],
                               scale=1.0 / D).then_inc(f_rt, 1)

        @block.gpsimd
        def _(pool):
            made = [0]

            def step():
                made[0] += 1
                pool.wait_ge(s_cst, made[0])

            pool.memset(ident[:, :], 0.0).then_inc(s_cst, 1)
            step()
            pool.memset(ones[:, :], 1.0).then_inc(s_cst, 1)
            step()
            pool.memset(ones_b[:, :], 1.0).then_inc(s_cst, 1)
            step()
            pool.memset(wdec[:, :], 0.0).then_inc(s_cst, 1)
            step()
            pool.memset(reset[:, :], 1.0).then_inc(s_cst, 1)
            step()
            pool.affine_select(out=ident[:, :], in_=ident[:, :], compare_op=ALU.not_equal, fill=1.0, base=0,
                               pattern=[[-1, 128]], channel_multiplier=1).then_inc(s_cst, 1)
            step()
            pool.affine_select(out=before_b[:, :], in_=ones_b[:, :], compare_op=ALU.is_ge, fill=0.0, base=-1,
                               pattern=[[1, 128]], channel_multiplier=-1).then_inc(s_cst, 1)
            step()
            pool.memset(reset[0:64, :].rearrange("p (n t) -> p n t", t=CH)[:, :, 0:1], 0.0).then_inc(s_cst, 1)
            step()
            pool.memset(reset[64:128, :].rearrange("p (n t) -> p n t", t=CH)[:, :, CH - 1:CH], 0.0).then_inc(s_cst, 1)
            step()
            kf, kb = W2["pf"], W2["pb"]
            for m, base_, cm, st in ((kf, 0, -1, 1), (kb, 0, 1, -1)):
                pool.memset(m[:, 0:128], 1.0).then_inc(s_cst, 1)
                step()
            for m, cm, st in ((kf, -1, 1), (kb, 1, -1)):
                v = m[:, 0:128]
                pool.affine_select(out=v, in_=v, compare_op=ALU.is_ge, fill=0.0, base=0,
                                   pattern=[[st, 128]], channel_multiplier=cm).then_inc(s_cst, 1)
                step()
            for m in (kf, kb):
                pool.memset(m[0:64, 64:128], 0.0).then_inc(s_cst, 1)
                step()
                pool.memset(m[64:128, 0:64], 0.0).then_inc(s_cst, 1)
                step()
            pool.tensor_copy(keep[:, 0, :], kf[:, 0:128]).then_inc(s_cst, 1)
            step()
            pool.tensor_copy(keep[:, 1, :], kb[:, 0:128]).then_inc(s_cst, 1)
            step()
            pool.memset(kf, 0.0).then_inc(s_cst, 1)
            step()
            pool.memset(kb, 0.0).then_inc(s_cst, 1)
            step()
            pool.memset(eps[:, :], EPS).then_inc(s_cst, 1)
            step()
            pool.memset(carry[:, :], 0.0).then_inc(s_cst, 1)
            step()
            pool.wait_ge(s_wz, 1)
            pool.tensor_tensor(wz_hl[:, 1], wz[:, :, :], wz_hl[:, 0].bitcast(f32), ALU.subtract).then_inc(s_wz, 1)

            def lo_halves(base, per, i, j):
                n = base + j
                rb = {SPL_PROJ_P: RAW_PROJ_P, SPL_OUT_P: RAW_OUT_P, SPL_PROJ_L: RAW_PROJ_L, SPL_OUT_L: RAW_OUT_L}[base]
                s = slot(rb, j)
                for q in range(2):
                    pool.wait_ge(s_hi, (2 * per) * i + (2 * n + q + 1) if not isinstance(i, int) or i else 2 * n + q + 1)
                    ins = pool.tensor_tensor(hl[:, s, 1, :, 128 * q:128 * q + 128], raw[:, s, :, 128 * q:128 * q + 128],
                                             hl[:, s, 0, :, 128 * q:128 * q + 128].bitcast(f32), ALU.subtract)
                    ins.then_inc(s_lo[s], 1)
                pool.wait_ge(s_lo[s], 2 * turn(base, per, i, j) + 2)
                pool.nop().then_inc(s_rawfree[s], 1)

            def stage2(b):
                base = SPL_PROJ_P if b.prompt else SPL_PROJ_L
                lo_halves(base, NPROJ, b.i, 0)
                lo_halves(base, NPROJ, b.i, 1)
                for t in range(b.NT):
                    b.wait(pool, s_hhi, t + 1)
                    pool.tensor_tensor(h_hl[:, 1, :, 128 * t:128 * t + 128],
                                       xn_t[:, t % 2, :].rearrange("p (k t) -> p k t", k=KC),
                                       h_hl[:, 0, :, 128 * t:128 * t + 128].bitcast(f32), ALU.subtract)\
                        .then_inc(s_hlo.sem, 1)
                for j in range(2, NPROJ):
                    lo_halves(base, NPROJ, b.i, j)
                for t in range(b.NT):
                    b.wait(pool, s_pf, t + 1)
                    b.wait(pool, s_pb, t + 1)
                    b.wait(pool, s_oi, t)
                    pool.tensor_tensor(W2["pp"], W2["pf"], W2["pb"], ALU.add).then_inc(s_pp.sem, 1)

            def stage3(b):
                base = SPL_OUT_P if b.prompt else SPL_OUT_L
                lo_halves(base, NOUT, b.i, 0)
                lo_halves(base, NOUT, b.i, 1)
                for k in range(8):
                    b.wait(pool, t_hi, k + 1)
                    name, o = ("o" if k < 4 else "c"), (k % 4) * b.T
                    pool.tensor_tensor(h_hl[:, 1, k, 0:b.T], W3[name][:, o:o + b.T],
                                       h_hl[:, 0, k, 0:b.T].bitcast(f32), ALU.subtract).then_inc(t_lo.sem, 1)
                lo_halves(base, NOUT, b.i, 2)
                lo_halves(base, NOUT, b.i, 3)

            p = Blk()
            stage2(p)
            stage_end(pool, 1, 2)
            stage3(p)
            pool.wait_ge(t_h2st.sem, 32)
            stage_end(pool, 2, 2)
            pool.memset(kf, 0.0).then_inc(s_cst, 1)
            pool.memset(kb, 0.0).then_inc(s_cst, 1)
            with pool.Fori(0, NBLK) as i:
                stage2(Blk(i))
            stage_end(pool, 3, 2)
            with pool.Fori(0, NBLK) as i:
                stage3(Blk(i))
            pool.wait_ge(t_h2st.sem, 16 * NTILE)
            stage_end(pool, 4, 2)
            pool.iota(W4["iota"], [[1, CAPL]], base=0, channel_multiplier=0,
                      allow_small_or_imprecise_dtypes=True).then_inc(s_cst, 1)
            idc = W4["idc"].bitcast(bf16).rearrange("p (t c) -> p t c", c=2)
            pool.iota(idc[:, :, 0], [[1, NTILE]], base=0, channel_multiplier=0,
                      allow_small_or_imprecise_dtypes=True).then_inc(s_cst, 1)
            pool.iota(idc[:, :, 1], [[0, NTILE]], base=0, channel_multiplier=1,
                      allow_small_or_imprecise_dtypes=True).then_inc(s_cst, 1)
            stage_end(pool, 5, 2)

            def gather(e, n_ids):
                pool.tensor_copy(ids_g[:, :], ids[:, e, :]).then_inc(e_ids, 1)
                wait_alone(pool, s_alone, e_ids, n_ids)
                for t, n in ((0, 128), (1, 128), (2, CAPP)):
                    pool.indirect_dma_start(xg[0:n, t, :], None, h2_rows[:, :],
                                            bass.IndirectOffsetOnAxis(ap=ids_g[0:n, t:t + 1], axis=0)).then_inc(e_gat, 16)

            def xe_lo(e, k):
                pool.wait_ge(e_xhi, 8 * e + (k + 1))
                pool.tensor_tensor(xe_hl[:, 1, k, :], h32e[:, k % 2, :], xe_hl[:, 0, k, :].bitcast(f32), ALU.subtract)\
                    .then_inc(e_xlo, 1)

            def expert(e, last):
                if not last:
                    pool.wait_ge(e_gat, 48 * e + 48)
                    pool.wait_ge(e_xk, 8 * e + 8)
                    pool.wait_ge(e_gate, e + 1)
                    gather(e + 1, 2 * e + 2)
                    for k in range(KC):
                        xe_lo(e + 1, k)
                wait_pos(pool, e_sc, 48 * e)
                pool.tensor_copy(ids_s[:, :], ids[:, e, :]).then_inc(e_ids, 1)
                wait_alone(pool, s_alone, e_ids, 2 * e + (2 if last else 3))
                wait_alone(pool, s_alone, e_yev, 8 * e + 8)
                for t, n in ((0, 128), (1, 128), (2, CAPP)):
                    pool.indirect_dma_start(x2_rows[:, :], bass.IndirectOffsetOnAxis(ap=ids_s[0:n, t:t + 1], axis=0),
                                            y_t[0:n, t, :], None, compute_op=ALU.add).then_inc(e_sc, 16)

            gather(0, 1)
            for k in range(KC):
                xe_lo(0, k)
            with pool.Fori(0, NE - 1) as e:
                expert(e, False)
            expert(NE - 1, True)
            pool.wait_ge(e_sc, 48 * NE)
            stage_end(pool, 6, 2)

        @block.tensor
        def _(pe):
            pe.wait_ge(s_vec, 16 * 16)
            pe.wait_ge(s_cst, 23)
            pe.transpose(psum[0][:, 0:NV], vecs[0:NV, :], ident[0:NV, 0:NV]).then_inc(s_vT, 1)
            for ct in range(4):
                last = pe.transpose(psum[1][:, 32 * ct:32 * ct + CW], w_cv[:, 128 * ct:128 * ct + 128],
                                    ident[0:CW, 0:CW])
            last.then_inc(s_vT, 1)

            def modulation(base, n, tile0, used):
                for j in range(n):
                    s = slot(base, j)
                    pe.wait_ge(s_raw[s], 16 * ((base + j) // 2 + 1))
                    for q in range(2):
                        o = 2 * (2 * j + q)
                        for k in range(KC):
                            last = pe.matmul(psum[7][:, o:o + 2], raw[:, s, k, 128 * q:128 * q + 128], scond[:, :, k],
                                             start=(k == 0), stop=(k == KC - 1))
                    last.then_inc(s_rawfree[s], 1)
                pe.drain().then_inc(s_mod, 1)

            pe.wait_ge(s_silc, 1)
            modulation(0, MOD1, 0, 0)
            pe.wait_ge(s_wz, 2)

            def three(out, lh, ll, rh, rl, first, last_):
                pe.matmul(out, lh, rh, start=first, stop=False)
                pe.matmul(out, lh, rl, start=False, stop=False)
                return pe.matmul(out, ll, rh, start=False, stop=last_)

            def unit(base, per, b, j, cols, values=False):
                s = slot(base, j)
                T = b.T
                if values:
                    pe.wait_ge(s_lo[s], 2 * turn(base, per, b.i, j) + 2)
                    for t in range(b.NT):
                        for k in range(KC):
                            a = h_hl[:, :, k, 128 * t:128 * t + 128]
                            last = three(psum[cols + t // 2][:, 256 * (t % 2):256 * (t % 2) + 256], a[:, 0], a[:, 1],
                                         hl[:, s, 0, k, :], hl[:, s, 1, k, :], k == 0, k == KC - 1)
                else:
                    for q in range(2):
                        pe.wait_ge(s_lo[s], 2 * turn(base, per, b.i, j) + q + 1)
                        for k in range(KC):
                            w = hl[:, s, :, k, 128 * q:128 * q + 128]
                            last = three(psum[cols + q][:, 0:T], w[:, 0], w[:, 1], h_hl[:, 0, k, 0:T],
                                         h_hl[:, 1, k, 0:T], k == 0, k == KC - 1)
                last.then_inc(s_unit, 1)

            def stage2(b):
                base = SPL_PROJ_P if b.prompt else SPL_PROJ_L
                T = b.T
                for t in range(b.NT):
                    b.wait(pe, s_xn, t + 1)
                    b.wait(pe, s_h32, t - 1)
                    if t < 2:
                        b.wait(pe, s_ue, 0)
                        b.wait(pe, s_pb, 0)
                        b.wait(pe, s_oe, 0)
                    for k in range(KC):
                        last = pe.transpose(psum[4 + 2 * (t % 2) + k // 4][:, 128 * (k % 4):128 * (k % 4) + 128],
                                            xn_t[:, t % 2, 128 * k:128 * k + 128], ident[:, :])
                    last.then_inc(s_xT.sem, 1)
                b.wait(pe, s_hlo, b.NT)
                b.wait(pe, s_h32, b.NT)
                for k in range(KC):
                    last = three(psum[4][0:2 * RANK, 0:T], wz_hl[:, 0, k, :], wz_hl[:, 1, k, :], h_hl[:, 0, k, 0:T],
                                 h_hl[:, 1, k, 0:T], k == 0, k == KC - 1)
                last.then_inc(s_z.sem, 1)
                b.wait(pe, s_r, -2)
                unit(base, NPROJ, b, 0, 0)
                b.wait(pe, s_zt, 1)
                for h in range(H):
                    pe.matmul(psum[4 + h][:, 0:T], wdec[:, 128 * h:128 * h + 128], W2["z"][0:2 * RANK, 0:T],
                              start=True, stop=True).then_inc(s_dec.sem, 1)
                b.wait(pe, s_r, 0)
                unit(base, NPROJ, b, 1, 2)
                for j, (sg_, n) in enumerate(((s_kfb, 1), (s_qfb, 1), (s_u, 2), (s_sg, 2), (s_u, 4), (s_sg, 4),
                                              (s_v, 1), (s_v, 2)), 2):
                    b.wait(pe, sg_, n)
                    unit(base, NPROJ, b, j, 2 * (j % 2), values=j in (6, 7))
                    if j == 7:
                        b.wait(pe, s_abs, 4)
                        b.wait(pe, s_min, 4)
                        gla(b, 0)
                    if j == 8:
                        gla(b, 1)
                for t in range(2, b.NT):
                    gla(b, t)

            def gla(b, t):
                T = b.T
                if t == 0:
                    b.wait(pe, s_dk, 3)
                b.wait(pe, s_ue, 2 * t)
                for h in range(H):
                    last = pe.transpose(psum[4][:, 128 * h:128 * h + 128],
                                        W2["A"][:, h * T + 128 * t:h * T + 128 * t + 128], ident[:, :])
                last.then_inc(s_kt.sem, 1)
                b.wait(pe, s_pb, t)
                for q, s in ((0, s_sf), (1, s_sb)):
                    for h in range(H):
                        o = h * T + 128 * t
                        last = pe.matmul(psum[5 + q][:, 128 * h:128 * h + 128],
                                         W2["C"][64 * q:64 * q + 64, o:o + 128],
                                         W2["B"][64 * q:64 * q + 64, o:o + 128], start=True, stop=True)
                    last.then_inc(s.sem, 1)
                b.wait(pe, s_kte, t + 1)
                b.wait(pe, s_v, 2)
                for q in range(2):
                    if q == 1:
                        b.wait(pe, s_pf, t + 1)
                    for h in range(H):
                        last = pe.matmul(psum[4 + q][:, 128 * h:128 * h + 128],
                                         W2["kT"][64 * q:64 * q + 64, 128 * h:128 * h + 128],
                                         v_t[64 * q:64 * q + 64, t, 128 * h:128 * h + 128], start=True, stop=True)
                    last.then_inc(s_upd.sem, 1)
                b.wait(pe, s_pp, t + 1)
                b.wait(pe, s_oe, t)
                for h in range(H):
                    last = pe.matmul(psum[7][:, 128 * h:128 * h + 128], v_t[:, t, 128 * h:128 * h + 128],
                                     W2["pp"][:, 128 * h:128 * h + 128], start=True, stop=True)
                last.then_inc(s_oi.sem, 1)

            def stage3(b):
                base = SPL_OUT_P if b.prompt else SPL_OUT_L
                T = b.T
                b.wait(pe, t_q, 16)
                b.wait(pe, t_S, 32)
                b.wait(pe, t_bs, b.NC)
                b.wait(pe, t_lg, 0)
                b.wait(pe, t_h2, 0)
                b.wait(pe, t_x2, 0)
                b.wait(pe, t_y, 0)
                for h in range(H):
                    for cc in range(b.NC):
                        last = pe.matmul(psum[h][:, 64 * cc:64 * cc + 64], S3[:, cc + 1, 128 * h:128 * h + 128],
                                         W3["q"][:, h * T + 64 * cc:h * T + 64 * cc + 64], start=True, stop=True)
                    last.then_inc(t_in.sem, 1)
                for h in range(H):
                    b.wait(pe, t_sq, h + 1)
                    pe.matmul(psum[4 + h][:, 0:T], ones[:, :], sq_t[:, h % 2, 0:T], start=True, stop=True)\
                        .then_inc(t_ms.sem, 1)
                b.wait(pe, t_c, 16)
                b.wait(pe, t_o1, 2)
                for ct in range(4):
                    last = pe.matmul(psum[0][:, 0:T], ones[:, :], W3["c"][:, ct * T:(ct + 1) * T], start=(ct == 0),
                                     stop=(ct == 3))
                last.then_inc(t_me.sem, 1)
                for ct in range(4):
                    b.wait(pe, t_csq, ct + 1)
                    last = pe.matmul(psum[1][:, 0:T], ones[:, :], sq_t[:, ct % 2, 0:T], start=(ct == 0), stop=(ct == 3))
                    last.then_inc(t_cs.sem, 1)
                b.wait(pe, t_cs, 4)
                pe.nop().then_inc(t_va.sem, 1)
                b.wait(pe, t_lo, 8)
                b.wait(pe, t_o1, 4)
                b.wait(pe, t_crt, 1)
                b.wait(pe, t_xc, 4)
                for j in range(NOUT):
                    if j >= 2:
                        b.wait(pe, t_y, j - 1)
                    unit(base, NOUT, b, j, 2 * (j % 2))
                b.wait(pe, t_y, 4)
                b.wait(pe, t_rt, 4)
                for t in range(b.NT):
                    b.wait(pe, t_x2, t)
                    for d in range(KC):
                        last = pe.transpose(psum[4 + d // 4][:, 128 * (d % 4):128 * (d % 4) + 128],
                                            W3["y"][:, d * T + 128 * t:d * T + 128 * t + 128], ident[:, :])
                    last.then_inc(t_yT.sem, 1)
                    b.wait(pe, t_xn, t + 1)
                    b.wait(pe, t_h2, t)
                    for d in range(KC):
                        last = pe.transpose(psum[6 + d // 4][:, 128 * (d % 4):128 * (d % 4) + 128],
                                            xn3[:, 128 * d:128 * d + 128], ident[:, :])
                    last.then_inc(t_xT.sem, 1)
                    b.wait(pe, t_h2, t + 1)
                    b.wait(pe, t_lg, t - 1)
                    for k in range(KC):
                        last = pe.matmul(psum[t % 2][:, 0:NE], h2T[:, k, :], wr[:, k, :], start=(k == 0),
                                         stop=(k == KC - 1))
                    last.then_inc(t_ro.sem, 1)

            p = Blk()
            pe.wait_ge(s_modv, 1)
            stage2(p)
            p.wait(pe, s_oe, p.NT)
            modulation(RAW_MOD2, MOD2, 16, 0)
            stage_end(pe, 1, 3)
            stage3(p)
            stage_end(pe, 2, 3)
            with pe.Fori(0, NBLK) as i:
                stage2(Blk(i))
            stage_end(pe, 3, 3)
            with pe.Fori(0, NBLK) as i:
                stage3(Blk(i))
            stage_end(pe, 4, 3)
            mb = W4["mb"].bitcast(bf16)
            with pe.Fori(0, 30) as i:
                pe.wait_ge(k_m, i + 1)
                pe.matmul(psum[0][:, 0:TE], ones_b[:, :], mb, start=True, stop=True).then_inc(k_cnt, 1)
            for n in range(2):
                pe.wait_ge(k_m, 31 + n)
                pe.matmul(psum[1][:, 0:TE], ones_b[:, :], mb, start=True, stop=True)
                pe.matmul(psum[2][:, 0:TE], before_b[:, :], mb, start=True, stop=True).then_inc(k_p, 1)
            idc = W4["idc"].bitcast(bf16).rearrange("p (t c) -> p t c", c=2)
            oh = W4["oh"].bitcast(bf16).rearrange("p (b s) -> p b s", b=2)
            with pe.Fori(0, NE) as e:
                wait_bank = e
                for t in range(NTILE):
                    pe.wait_ge(k_oh, NTILE * e + (t + 1))
                    if t < 2:
                        last = pe.matmul(psum[5][0:CAPP, 0:2], oh[:, t % 2, 0:CAPP], idc[:, t, :], start=(t == 0),
                                         stop=(t == 1))
                    else:
                        pe.matmul(psum[3][:, 0:2], oh[:, t % 2, 0:128], idc[:, t, :], start=(t == 2),
                                  stop=(t == NTILE - 1))
                        last = pe.matmul(psum[4][:, 0:2], oh[:, t % 2, 128:256], idc[:, t, :], start=(t == 2),
                                         stop=(t == NTILE - 1))
                    last.then_inc(k_id, 1)
            stage_end(pe, 5, 3)

            def gather_T(e, k):
                if k == 0:
                    pe.wait_ge(e_gat, 48 * e + 48)
                wait_pos(pe, e_xh, 8 * e + max(k - 1, 0))
                for t, n in ((0, 128), (1, 128), (2, CAPP)):
                    last = pe.transpose(psum[4 + k % 2][:, 128 * t:128 * t + n], xg[0:n, t, 128 * k:128 * k + 128],
                                        ident[0:n, 0:n])
                last.then_inc(e_xk, 1)

            def out_T(e, d):
                pe.wait_ge(e_yT, 8 * e + (d + 1))
                wait_pos(pe, e_yev, 8 * e + max(d - 1, 0))
                for t, n in ((0, 128), (1, 128), (2, CAPP)):
                    last = pe.transpose(psum[6 + d % 2][0:n, 128 * t:128 * t + 128],
                                        yT_t[:, d % 4, 128 * t:128 * t + n], ident[:, :])
                last.then_inc(e_yt, 1)

            def expert(e, last_e):
                for j in range(NEXP):
                    s = j % 2
                    if j < 8:
                        rhs, bank = xe_hl, (0 if j % 2 == 0 else 2)
                    else:
                        rhs, bank = he_hl, 2 * (j % 2)
                    for q in range(2):
                        pe.wait_ge(s_lo[s], NEXP * e + (2 * ((SPL_EXP + j) // 2) + q + 1))
                        if j == 0 or j == 1:
                            wait_pos(pe, e_yT, 8 * e)
                        elif j < 8:
                            pe.wait_ge(e_si if j % 2 == 0 else e_h, 8 * e + 2 * (j // 2))
                        elif j == 8:
                            pe.wait_ge(e_si, 8 * e + 8)
                        elif j == 9:
                            pe.wait_ge(e_h, 8 * e + 8)
                        else:
                            pe.wait_ge(e_yT, 8 * e + (2 * (j - 9)))
                        for k in range(KC):
                            if j == 0 and q == 0:
                                pe.wait_ge(e_xlo, 8 * e + (k + 1))
                            if j == 8 and q == 0:
                                pe.wait_ge(e_hlo, 8 * e + (k + 1))
                            w = hl[:, s, :, k, 128 * q:128 * q + 128]
                            last = three(psum[bank + q][:, 0:CAP], w[:, 0], w[:, 1], rhs[:, 0, k, :], rhs[:, 1, k, :],
                                         k == 0, k == KC - 1)
                    last.then_inc(s_unit, 1)
                    if j >= 9:
                        out_T(e, 2 * (j - 9))
                        out_T(e, 2 * (j - 9) + 1)
                    if j >= 8 and not last_e:
                        gather_T(e + 1, 2 * (j - 8))
                        gather_T(e + 1, 2 * (j - 8) + 1)
                out_T(e, 6)
                out_T(e, 7)

            for k in range(KC):
                gather_T(0, k)
            with pe.Fori(0, NE - 1) as e:
                expert(e, False)
            expert(NE - 1, True)
            stage_end(pe, 6, 3)

        @block.vector
        def _(dve):
            dve.wait_ge(s_cst, 23)
            dve.wait_ge(s_vT, 1)
            dve.tensor_copy(col[:, 0:NV], psum[0][:, 0:NV]).then_inc(s_col, 1)
            dve.wait_ge(s_vT, 2)
            dve.tensor_copy(wcv[:, :, :], psum[1][:, 0:128].rearrange("p (c w) -> p c w", c=4)[:, :, 0:CW])\
               .then_inc(s_col, 1)
            dve.wait_ge(s_col, 2)

            def mod_vectors(n, t0, cnt):
                dve.wait_ge(s_mod, n)
                m0, g, A = (8, V_GM, A1) if n == 1 else (32, V_GF, A2)
                bias = col[:, V_BM + t0:V_BM + t0 + cnt].unsqueeze(2).broadcast_to([128, cnt, 2])
                dve.tensor_tensor(mod[:, t0:t0 + cnt, :], psum[7][:, 0:2 * cnt].rearrange("p (t c) -> p t c", c=2),
                                  bias, ALU.add).then_inc(s_vconst, 1)
                dve.wait_ge(s_vconst, 2 * n - 1)
                dve.tensor_scalar(A[:, :, :], mod[:, m0:m0 + 8, :], 1.0, None, ALU.add).then_inc(s_vconst, 1)
                dve.wait_ge(s_vconst, 2 * n)
                dve.tensor_tensor(A[:, :, :], A[:, :, :], col[:, g:g + 8].unsqueeze(2).broadcast_to([128, 8, 2]),
                                  ALU.mult).then_inc(s_modv, 1)
                dve.wait_ge(s_modv, n)

            mod_vectors(1, 0, 16)

            def stage2(b):
                T, NC = b.T, b.NC
                n = 0 if b.prompt else b.i + 1
                A, B, C = (W2[x][:, 0:H * T] for x in "ABC")
                for t in range(b.NT):
                    b.wait(dve, s_rt, t + 1)
                    dve.reciprocal(stat[:, 8 + t:9 + t], stat[:, 4 + t:5 + t]).then_inc(s_rstd.sem, 1)
                    if t >= 1:
                        modulate(b, t - 1)
                modulate(b, b.NT - 1)
                b.wait(dve, s_kt, 0)
                for h in range(H):
                    b.wait(dve, s_dec, h + 1)
                    dve.tensor_scalar(A[:, h * T:(h + 1) * T], psum[4 + h][:, 0:T], col[:, V_BD + h:V_BD + h + 1], 0.0,
                                      ALU.add, ALU.min).then_inc(s_min.sem, 1)
                b.wait(dve, s_min, 4)
                b.wait(dve, s_ln, 2)
                dve.tensor_tensor(A, A, B, ALU.subtract).then_inc(s_g.sem, 1)
                b.wait(dve, s_g, 1)
                b.wait(dve, s_sb, 0)
                rs = reset[:, 0:H * T]
                dve.tensor_tensor_scan(C[0:64], rs[0:64], A[0:64], 0.0, ALU.mult, ALU.add).then_inc(s_cum.sem, 1)
                dve.tensor_tensor_scan(C[64:128, ::-1], rs[64:128, ::-1], A[64:128, ::-1], 0.0, ALU.mult, ALU.add)\
                   .then_inc(s_cum.sem, 1)
                b.wait(dve, s_cum, 2)
                b.wait(dve, s_D, 0)
                cl = W2["cl"][:, 0:H * NC]
                cv = C.rearrange("p (n t) -> p n t", t=CH)
                dve.tensor_copy(cl[0:64], cv[0:64, :, CH - 1]).then_inc(s_cl.sem, 1)
                dve.tensor_copy(cl[64:128], cv[64:128, :, 0]).then_inc(s_cl.sem, 1)
                b.wait(dve, s_cl, 2)
                dve.tensor_tensor(A.rearrange("p (n t) -> p n t", t=CH),
                                  cl.unsqueeze(2).broadcast_to([128, H * NC, CH]), cv, ALU.subtract)\
                   .then_inc(s_cl.sem, 1)
                b.wait(dve, s_kfb, 1)
                b.wait(dve, s_ex, 2)
                dve.tensor_tensor(A, A, W2["k"][:, 0:H * T], ALU.mult).then_inc(s_dk.sem, 1)
                b.wait(dve, s_ex, 3)
                dve.tensor_tensor(C, C, W2["k"][:, 0:H * T], ALU.mult).then_inc(s_dk.sem, 1)
                b.wait(dve, s_qfb, 1)
                dve.tensor_tensor(B, B, W2["q"][:, 0:H * T], ALU.mult).then_inc(s_dk.sem, 1)
                b.wait(dve, s_sst, 0)
                if b.prompt:
                    dve.wait_ge(s_cst, 23)
                dve.tensor_copy(S_t[0:64, 0, :], carry[0:64, :]).then_inc(s_c0.sem, 1)
                glu(b, 0)
                for w in range(CW // 2):
                    taps(b, 0, w)
                glu(b, 2)
                for w in range(CW // 2, CW):
                    taps(b, 0, w)
                per = -(-CW // b.NT)
                for t in range(b.NT):
                    gla(b, t)
                    for w in range(per * t, min(CW, per * t + per)):
                        taps(b, 1, w)
                b.wait(dve, s_fs, NC)
                dve.tensor_copy(carry[0:64, :], S_t[0:64, NC, :]).then_inc(s_c1.sem, 1)

            def modulate(b, t):
                b.wait(dve, s_xT, t + 1)
                for k in range(KC):
                    last = dve.tensor_scalar(xn_t[:, t % 2, 128 * k:128 * k + 128],
                                             psum[4 + 2 * (t % 2) + k // 4][:, 128 * (k % 4):128 * (k % 4) + 128],
                                             A1[:, k, b.cond:b.cond + 1], mod[:, k, b.cond:b.cond + 1],
                                             ALU.mult, ALU.add)
                last.then_inc(s_h32.sem, 1)

            def glu(b, ct):
                for q in range(2):
                    b.wait(dve, s_sg, ct + q + 1)
                    uu = W2["u"][:, (ct + q) * BT:(ct + q) * BT + b.T]
                    dve.tensor_tensor(uu, psum[q][:, 0:b.T], uu, ALU.mult).then_inc(s_u.sem, 1)

            ORDER = [CW // 2] + [w for w in range(CW) if w != CW // 2]

            def taps(b, pair, n):
                w = ORDER[n]
                off = w - CW // 2
                rl = b.T if b.prompt else GRID
                for q in range(2):
                    ct = 2 * pair + q
                    uu = W2["u"][:, ct * BT:ct * BT + b.T].rearrange("p (r t) -> p r t", t=rl)
                    ac = W2["acc"][:, ct * b.T:(ct + 1) * b.T].rearrange("p (r t) -> p r t", t=rl)
                    done = 2 * CW * pair + 2 * n + q
                    if n == 0:
                        b.wait(dve, s_u, ct + 1)
                        b.wait(dve, s_cstr, 0)
                        dve.tensor_scalar(ac, uu, wcv[:, ct, w:w + 1], col[:, V_CB + ct:V_CB + ct + 1], ALU.mult,
                                          ALU.add).then_inc(s_conv.sem, 1)
                        continue
                    b.wait(dve, s_conv, done - 1)
                    a0, a1 = max(0, -off), rl - max(0, off)
                    dve.scalar_tensor_tensor(out=ac[:, :, a0:a1], in0=uu[:, :, a0 + off:a1 + off],
                                             scalar=wcv[:, ct, w:w + 1], in1=ac[:, :, a0:a1], op0=ALU.mult,
                                             op1=ALU.add).then_inc(s_conv.sem, 1)

            def gla(b, t):
                n = 0 if b.prompt else b.i + 1
                for q, s, d, name in ((0, s_sf, s_pf, "pf"), (1, s_sb, s_pb, "pb")):
                    b.wait(dve, s_pp, t)
                    if t == 0:
                        dve.wait_ge(s_cst, 23 if b.prompt else 25)
                    wait_alone(dve, s_alone, s.sem, b.at(s, t + 1))
                    dve.copy_predicated(W2[name].rearrange("p (h i) -> p h i", h=H),
                                    keep[:, q, :].unsqueeze(1).broadcast_to([128, H, 128]),
                                    psum[5 + q][:, :].rearrange("p (h i) -> p h i", h=H)).then_inc(d.sem, 1)
                for cc in (2 * t, 2 * t + 1):
                    b.wait(dve, s_ue, cc + 1)
                    b.wait(dve, s_D, 1)
                    b.wait(dve, s_fs, cc)
                    if cc == 0:
                        b.wait(dve, s_c0, 1)
                    for h in range(H):
                        last = dve.scalar_tensor_tensor(
                            out=S_t[0:64, cc + 1, 128 * h:128 * h + 128], in0=S_t[0:64, cc, 128 * h:128 * h + 128],
                            scalar=dec[0:64, n, h, cc:cc + 1], in1=S_t[0:64, cc + 1, 128 * h:128 * h + 128],
                            op0=ALU.mult, op1=ALU.add)
                    last.then_inc(s_fs.sem, 1)

            def stage3(b):
                T, NC = b.T, b.NC
                n = 0 if b.prompt else NBLK - b.i
                b.wait(dve, t_S, 32)
                dve.tensor_copy(S3[64:128, NC, :], carry[64:128, :]).then_inc(t_c0.sem, 1)
                b.wait(dve, t_c0, 1)
                for m, cc in enumerate(reversed(range(NC))):
                    if not (b.prompt and m == 0):
                        wait_alone(dve, s_alone, t_bs.sem, b.at(t_bs, m))
                    for h in range(H):
                        last = dve.scalar_tensor_tensor(
                            out=S3[64:128, cc, 128 * h:128 * h + 128], in0=S3[64:128, cc + 1, 128 * h:128 * h + 128],
                            scalar=dec[64:128, n, h, cc:cc + 1], in1=S3[64:128, cc, 128 * h:128 * h + 128],
                            op0=ALU.mult, op1=ALU.add)
                    last.then_inc(t_bs.sem, 1)
                b.wait(dve, t_bs, NC)
                dve.tensor_copy(carry[64:128, :], S3[64:128, 0, :]).then_inc(t_c1.sem, 1)
                b.wait(dve, t_o, 16)
                for h in range(H):
                    b.wait(dve, t_in, h + 1)
                    o = W3["o"][:, h * T:(h + 1) * T]
                    dve.tensor_tensor(o, psum[h][:, 0:T], o, ALU.add).then_inc(t_o1.sem, 1)
                b.wait(dve, t_c, 16)
                b.wait(dve, t_me, 1)
                for ct in range(4):
                    x = W3["c"][:, ct * T:(ct + 1) * T]
                    dve.scalar_tensor_tensor(out=x, in0=psum[0][:, 0:T], scalar=-1.0 / 512, in1=x, op0=ALU.mult,
                                             op1=ALU.add).then_inc(t_xc.sem, 1)
                b.wait(dve, t_r, 16)
                for h in range(H):
                    o = W3["o"][:, h * T:(h + 1) * T]
                    r = rs_t[:, h % 2, 0:T]
                    b.wait(dve, t_rt, h + 1)
                    dve.reciprocal(r, r).then_inc(t_rc.sem, 1)
                    b.wait(dve, t_rc, h + 1)
                    b.wait(dve, t_o1, h + 1)
                    b.wait(dve, t_sq, h + 1)
                    dve.tensor_tensor(o, o, r, ALU.mult).then_inc(t_on.sem, 1)
                    b.wait(dve, t_on, h + 1)
                    dve.scalar_tensor_tensor(out=o, in0=o, scalar=col[:, V_GN:V_GN + 1],
                                             in1=W3["r"][:, h * T:(h + 1) * T], op0=ALU.mult, op1=ALU.mult)\
                       .then_inc(t_og.sem, 1)
                b.wait(dve, t_crt, 1)
                dve.reciprocal(rs_t[:, 0, 0:T], rs_t[:, 0, 0:T]).then_inc(t_crc.sem, 1)
                b.wait(dve, t_crc, 1)
                b.wait(dve, t_csq, 4)
                for ct in range(4):
                    x = W3["c"][:, ct * T:(ct + 1) * T]
                    b.wait(dve, t_xc, ct + 1)
                    dve.tensor_tensor(x, x, rs_t[:, 0, 0:T], ALU.mult).then_inc(t_cn.sem, 1)
                for t in range(b.NT):
                    b.wait(dve, t_yT, t + 1)
                    b.wait(dve, t_x[t % 2], 16 * (t // 2 + 1))
                    for q in range(2):
                        last = dve.tensor_tensor(x3[:, t % 2, 512 * q:512 * q + 512], psum[4 + q][:, :],
                                                 x3[:, t % 2, 512 * q:512 * q + 512], ALU.add)
                    last.then_inc(t_x2.sem, 1)
                    b.wait(dve, t_r2, t + 1)
                    dve.reciprocal(stat[:, 8 + t:9 + t], stat[:, 4 + t:5 + t]).then_inc(t_i2.sem, 1)
                    b.wait(dve, t_xT, t + 1)
                    b.wait(dve, t_ro, t)
                    for k in range(KC):
                        last = dve.tensor_scalar(h2T[:, k, :], psum[6 + k // 4][:, 128 * (k % 4):128 * (k % 4) + 128],
                                                 A2[:, k, b.cond:b.cond + 1], mod[:, 24 + k, b.cond:b.cond + 1],
                                                 ALU.mult, ALU.add)
                    last.then_inc(t_h2.sem, 1)
                    wait_alone(dve, s_alone, t_ro.sem, b.at(t_ro, t + 1))
                    gt = t if b.prompt else (NBLK - 1 - b.i) * (BT // 128) + (TP // 128 + t)
                    dst = logits[:, gt, :] if b.prompt else logits[:, bass.ds(gt, 1), :].squeeze(1)
                    dve.tensor_copy(dst, psum[t % 2][:, 0:NE]).then_inc(t_lg.sem, 1)

            p = Blk()
            stage2(p)
            mod_vectors(2, 16, 32)
            stage_end(dve, 1, 4)
            stage3(p)
            stage_end(dve, 2, 4)
            dve.wait_ge(s_st, 64)
            with dve.Fori(0, NBLK) as i:
                stage2(Blk(i))
            stage_end(dve, 3, 4)
            with dve.Fori(0, NBLK) as i:
                stage3(Blk(i))
            stage_end(dve, 4, 4)

            link_n = [0]

            def link(ins):
                link_n[0] += 1
                ins.then_inc(k_v, 1)
                dve.wait_ge(k_v, link_n[0])

            def te(name):
                return W4[name].rearrange("p (t e) -> p t e", e=NE)

            aff = te("aff")
            link(dve.tensor_reduce(W4["mx"], logits[:, :, :], AX.X, ALU.max))
            link(dve.tensor_tensor(aff, logits[:, :, :], W4["mx"].unsqueeze(2).broadcast_to([128, NTILE, NE]),
                                   ALU.subtract))
            dve.wait_ge(k_e, 1)
            link(dve.tensor_reduce(W4["sm"], aff, AX.X, ALU.add))
            link(dve.reciprocal(W4["sm"], W4["sm"]))
            link(dve.tensor_tensor(aff, aff, W4["sm"].unsqueeze(2).broadcast_to([128, NTILE, NE]), ALU.mult))
            link(dve.memset(W4["kk"][:, 0:NE], float(CAPP)))
            link(dve.memset(W4["kk"][:, NE:2 * NE], float(CAPL)))
            thr, cand, bit, kp = (W4[x].bitcast(u32) for x in ("thr", "cand", "bit", "kp"))
            link(dve.memset(W4["thr"], 0.0))
            link(dve.memset(bit, 1 << 29))
            cnt, need = W4["cnt"], W4["need"]
            mb = W4["mb"].bitcast(bf16)
            PT = TP // 128
            sets = ((0, PT, 0), (PT, NTILE, 1))

            def per_set(out, op, src, values_):
                for a, z, s in sets:
                    v = values_[:, NE * s:NE * s + NE].unsqueeze(1).broadcast_to([128, z - a, NE])
                    ins = dve.tensor_tensor(out[:, a:z, :], src[:, a:z, :], v, op)
                return ins

            mb3 = mb.rearrange("p (t e) -> p t e", e=NE)
            base = link_n[0]
            PER = 5
            with dve.Fori(0, 30) as i:
                def step(j, ins):
                    ins.then_inc(k_v, 1)
                    wait_alone(dve, s_alone, k_v, PER * i + (base + j))
                step(1, dve.tensor_tensor(cand, thr, bit, ALU.bitwise_or))
                per_set(mb3, ALU.is_ge, aff, W4["cand"]).then_inc(k_m, 1)
                dve.wait_ge(k_cnt, i + 1)
                for a, z, s in sets:
                    ins = dve.tensor_reduce(cnt[:, NE * s:NE * s + NE],
                                            psum[0][:, NE * a:NE * z].rearrange("p (t e) -> p e t", e=NE), AX.X,
                                            ALU.add)
                step(2, ins)
                step(3, dve.tensor_tensor(kp, cnt, W4["kk"], ALU.is_ge))
                step(4, dve.copy_predicated(thr, kp, cand))
                step(5, dve.tensor_scalar(bit, bit, 1, None, ALU.logical_shift_right))
            link_n[0] = base + PER * 30
            per_set(te("sel"), ALU.is_gt, aff, W4["thr"])
            link(per_set(te("eq"), ALU.is_equal, aff, W4["thr"]))

            rst = W4["rst"].rearrange("p (e t) -> p e t", e=NE)
            link(dve.memset(W4["rst"], 1.0))
            dve.memset(rst[:, :, 0:1], 0.0)
            link(dve.memset(rst[:, :, PT:PT + 1], 0.0))
            tot, inc = W4["tot"], W4["inc"]

            def rank(out, n):
                dve.wait_ge(k_p, n)
                link(dve.tensor_copy(tot.rearrange("p (e t) -> p e t", e=NE),
                                     psum[1][:, 0:TE].rearrange("p (t e) -> p e t", e=NE)))
                link(dve.tensor_tensor_scan(inc, W4["rst"], tot, 0.0, ALU.mult, ALU.add))
                link(dve.tensor_tensor(inc, inc, tot, ALU.subtract))
                link(dve.tensor_tensor(out, psum[2][:, 0:TE].rearrange("p (t e) -> p t e", e=NE),
                                       inc.rearrange("p (e t) -> p t e", e=NE), ALU.add))

            dve.tensor_copy(mb, W4["eq"]).then_inc(k_m, 1)
            rank(te("pos"), 1)
            dve.tensor_copy(mb, W4["sel"]).then_inc(k_m, 1)
            dve.wait_ge(k_p, 2)
            for a, z, s in sets:
                ins = dve.tensor_reduce(cnt[:, NE * s:NE * s + NE],
                                        psum[1][:, NE * a:NE * z].rearrange("p (t e) -> p e t", e=NE), AX.X, ALU.add)
            link(ins)
            link(dve.tensor_tensor(need, W4["kk"], cnt, ALU.subtract))
            link(per_set(te("t1"), ALU.is_lt, te("pos"), need))
            link(dve.tensor_tensor(W4["t1"], W4["t1"], W4["eq"], ALU.mult))
            dve.tensor_copy(W4["t2"], W4["pos"])
            rank(te("pos"), 2)
            link(per_set(te("t2"), ALU.add, te("t2"), cnt))
            link(dve.tensor_tensor(W4["t2"], W4["t2"], W4["t1"], ALU.mult))
            link(dve.tensor_tensor(W4["pos"], W4["pos"], W4["sel"], ALU.mult))
            link(dve.tensor_tensor(W4["pos"], W4["pos"], W4["t2"], ALU.add))
            link(dve.tensor_tensor(W4["sel"], W4["sel"], W4["t1"], ALU.add))
            link(dve.tensor_scalar(W4["sel"], W4["sel"], -1.0, 4096.0, ALU.add, ALU.mult))
            link(dve.tensor_tensor(W4["pos"], W4["pos"], W4["sel"], ALU.add))
            link(dve.memset(ids[:, :, :], 0))
            dve.wait_ge(s_cst, 28)
            oh = W4["oh"].bitcast(bf16).rearrange("p (b s) -> p b s", b=2)
            idf = W4["idf"].rearrange("p (t c) -> p t c", c=2)
            base2 = link_n[0]
            with dve.Fori(0, NE) as e:
                for t in range(NTILE):
                    if t >= 2:
                        dve.wait_ge(k_id, NTILE * e + (t - 1))
                    cap = CAPP if t < PT else CAPL
                    pos_e = te("pos")[:, t, bass.ds(e, 1)]
                    dve.tensor_scalar(oh[:, t % 2, 0:cap], W4["iota"][:, 0:cap], pos_e, None,
                                      ALU.is_equal).then_inc(k_oh, 1)
                dve.wait_ge(k_id, NTILE * e + NTILE)
                for s, n in ((0, 128), (1, 128), (2, CAPP)):
                    ins = dve.tensor_copy(idf[0:n, s, :], psum[3 + s][0:n, 0:2])
                ins.then_inc(k_ev, 1)
                dve.wait_ge(k_ev, 2 * e + 1)
                for s, n in ((0, 128), (1, 128), (2, CAPP)):
                    ins = dve.scalar_tensor_tensor(out=ids[0:n, bass.ds(e, 1), s], in0=idf[0:n, s, 0:1], scalar=128.0,
                                                   in1=idf[0:n, s, 1:2], op0=ALU.mult, op1=ALU.add)
                ins.then_inc(k_ev, 1)
                wait_alone(dve, s_alone, k_ev, 2 * e + 2)
            stage_end(dve, 5, 4)

            def elo(e, j):
                s = j % 4
                src = raw[:, s] if s < 2 else raw2[:, s - 2]
                for q in range(2):
                    dve.wait_ge(s_hi, 2 * NEXP * e + (2 * (SPL_EXP + j) + q + 1))
                    dve.tensor_tensor(hl[:, j % 2, 1, :, 128 * q:128 * q + 128], src[:, :, 128 * q:128 * q + 128],
                                      hl[:, j % 2, 0, :, 128 * q:128 * q + 128].bitcast(f32), ALU.subtract)\
                       .then_inc(s_lo[j % 2], 1)

            def gather_mod(e, k):
                dve.wait_ge(e_xk, 8 * e + (k + 1))
                wait_pos(dve, e_xlo, 8 * e + max(k - 1, 0))
                for a, z, cnd in ((0, CAPL, 1), (CAPL, CAP, 0)):
                    last = dve.tensor_scalar(h32e[:, k % 2, a:z], psum[4 + k % 2][:, a:z], A2[:, k, cnd:cnd + 1],
                                             mod[:, 24 + k, cnd:cnd + 1], ALU.mult, ALU.add)
                last.then_inc(e_xh, 1)

            def gate_cols(e):
                dve.wait_ge(e_gat, 48 * e + 48)
                wait_pos(dve, e_yev, 8 * e)
                for s, n in ((0, 128), (1, 128), (2, CAPP)):
                    src = xg[0:n, s, D:D + NE][:, bass.ds(e, 1)] if not isinstance(e, int) else \
                        xg[0:n, s, D + e:D + e + 1]
                    last = dve.tensor_copy(gate_t[0:n, s:s + 1], src)
                last.then_inc(e_gate, 1)

            def out_rows(e, d):
                dve.wait_ge(e_yt, 8 * e + (d + 1))
                if d == 0:
                    wait_pos(dve, e_sc, 48 * e)
                    dve.wait_ge(e_gate, e + 1)
                for s, n in ((0, 128), (1, 128), (2, CAPP)):
                    last = dve.tensor_scalar(y_t[0:n, s, 128 * d:128 * d + 128],
                                             psum[6 + d % 2][0:n, 128 * s:128 * s + 128], gate_t[0:n, s:s + 1], None,
                                             ALU.mult)
                last.then_inc(e_yev, 1)

            def expert(e, last_e):
                gate_cols(e)
                for j in range(NEXP):
                    if j + 2 < NEXP or not last_e:
                        elo(e, j + 2)
                    if j < 8 and j % 2 == 1:
                        for q in range(2):
                            ft = j - 1 + q
                            dve.wait_ge(e_si, 8 * e + (ft + 1))
                            dve.wait_ge(s_unit, NEXP * e + (SPL_EXP + j + 1))
                            wait_pos(dve, e_hlo, 8 * e + max(ft - 1, 0))
                            dve.tensor_tensor(hx_t[:, ft % 2, :], psum[2 + q][:, 0:CAP], sg_t[:, ft % 2, :], ALU.mult)\
                               .then_inc(e_h, 1)
                        for q in range(2):
                            ft = j - 1 + q
                            dve.wait_ge(e_hhi, 8 * e + (ft + 1))
                            dve.tensor_tensor(he_hl[:, 1, ft, :], hx_t[:, ft % 2, :], he_hl[:, 0, ft, :].bitcast(f32),
                                              ALU.subtract).then_inc(e_hlo, 1)
                    if j >= 9:
                        out_rows(e, 2 * (j - 9))
                        out_rows(e, 2 * (j - 9) + 1)
                    if j >= 8 and not last_e:
                        gather_mod(e + 1, 2 * (j - 8))
                        gather_mod(e + 1, 2 * (j - 8) + 1)
                out_rows(e, 6)
                out_rows(e, 7)

            for k in range(KC):
                gather_mod(0, k)
            elo(0, 0)
            elo(0, 1)
            with dve.Fori(0, NE - 1) as e:
                expert(e, False)
            expert(NE - 1, True)
            stage_end(dve, 6, 4)
            dve.wait_ge(f_g, 16)
            for t in range(NTILE):
                dve.wait_ge(f_rt, t + 1)
                dve.reciprocal(stat[:, 16 + t % 8:17 + t % 8], stat[:, 8 + t % 8:9 + t % 8]).then_inc(f_rc, 1)
                dve.wait_ge(f_rc, t + 1)
                if t >= 4:
                    dve.wait_ge(f_st[t % 4], 16 * (t // 4))
                dve.scalar_tensor_tensor(out=y6[:, t % 4, :], in0=x6[:, t % 4, :], scalar=stat[:, 16 + t % 8:17 + t % 8],
                                         in1=W6["g"], op0=ALU.mult, op1=ALU.mult).then_inc(f_y, 1)


_INS = ['x_prompt', 'x_sample', 'state_gla_fwd', 'state_gla_bwd', 'c', 'c_ctx', 'norm_mix_g', 'norm_ffn_g',
        'norm_final_g', 'w_mod', 'b_mod', 'w_in', 'w_decay_f', 'b_decay_f', 'w_decay_b', 'b_decay_b', 'gla_norm_g',
        'conv_w', 'conv_b', 'conv_ln_g', 'conv_ln_b', 'w_out', 'w_router', 'w_e_gate', 'w_e_up', 'w_e_down']
_OUTS = [((1, TP, D), 'float32'), ((1, TL, D), 'float32'), ((1, 1, H, DK, DV), 'float32'),
         ((1, 1, H, DK, DV), 'float32')]


def kernel(**inputs):
    import numpy as _np
    import concourse.bacc as _bacc
    from concourse import mybir as _mybir
    from concourse.bass_utils import run_bass_kernel_spmd as _run

    nc = _bacc.Bacc("TRN2", target_bir_lowering=False, num_devices=1)
    arrays, args = {}, []
    for name in _INS:
        a = _np.ascontiguousarray(inputs[name])
        arrays[f"in_{name}_dram"] = a
        args.append(nc.dram_tensor(f"in_{name}_dram", a.shape, _mybir.dt.from_np(a.dtype), kind="ExternalInput").ap())
    for i, (shape, dtype) in enumerate(_OUTS):
        dt = _mybir.dt.from_np(_np.dtype(dtype))
        args.append(nc.dram_tensor(f"out_{i}_dram", shape, dt, kind="ExternalOutput").ap())
    hybrid_layer(nc, *args)
    r = _run(nc, [arrays], core_ids=[0])
    return tuple(r.results[0][f"out_{i}_dram"] for i in range(len(_OUTS)))
```

```python
import concourse.bass as bass
from concourse import mybir
from contextlib import ExitStack

D = 1024
KC = D // 128
TP, TL = 256, 2048
NTOK = TP + TL
NTILE = NTOK // 128
BT = 512
NBLK = TL // BT
H, DK, DV, CH = 4, 64, 128, 64
RANK = 16
CW = 31
GRID = 64
NE, DE = 16, 1024
CAPP, CAPL = 2 * TP // NE, 2 * TL // NE
CAP = CAPL + CAPP
EPS = 1e-6
TAU = 16.0
OQ, OK, OV, OR, OZ, OGA, OGG = 0, 256, 512, 1024, 1536, 1568, 2080
PROJ_COLS = [OK, OQ, OGA, OGG, OGA + 256, OGG + 256, OV, OV + 256, OR, OR + 256]
NPROJ, NOUT, NEXP = len(PROJ_COLS), 4, 12
MOD1, MODB = 8, 4
RAW_PROJ_P = 0
RAW_PROJ_L = RAW_PROJ_P + NPROJ
RAW_OUT_P = RAW_PROJ_L + (NPROJ + MODB) * NBLK
RAW_OUT_L = RAW_OUT_P + NOUT
SPL_PROJ_P = 0
SPL_PROJ_L = SPL_PROJ_P + NPROJ
SPL_OUT_P = SPL_PROJ_L + NPROJ * NBLK
SPL_OUT_L = SPL_OUT_P + NOUT
SPL_EXP = SPL_OUT_L + NOUT * NBLK
RAW_OF = {SPL_PROJ_P: (RAW_PROJ_P, NPROJ), SPL_PROJ_L: (RAW_PROJ_L, NPROJ + MODB),
          SPL_OUT_P: (RAW_OUT_P, NOUT), SPL_OUT_L: (RAW_OUT_L, NOUT)}


class Sig:

    def __init__(self, sem, p, l=None):
        self.sem, self.p, self.l = sem, p, p if l is None else l


def wait_alone(eng, settled, sem, value):
    eng.wait_ge(sem, value)
    eng.sem_inc(settled, 1)


class Blk:

    def __init__(self, i=None, settled=None):
        self.settled = settled
        self.prompt = i is None
        self.i = 0 if i is None else i
        self.T = TP if self.prompt else BT
        self.NT = self.T // 128
        self.NC = self.T // CH
        self.cond = 0 if self.prompt else 1

    def at(self, sig, j):
        return j if self.prompt else self.i * sig.l + (sig.p + j)

    def wait(self, eng, sig, j):
        v = self.at(sig, j)
        if isinstance(v, int) and v <= 0:
            return
        if self.settled is None:
            eng.wait_ge(sig.sem, v)
        else:
            wait_alone(eng, self.settled, sig.sem, v)


def hybrid_layer(nc, x_prompt, x_sample, state_gla_fwd, state_gla_bwd, c, c_ctx, norm_mix_g, norm_ffn_g,
                 norm_final_g, w_mod, b_mod, w_in, w_decay_f, b_decay_f, w_decay_b, b_decay_b, gla_norm_g,
                 conv_w, conv_b, conv_ln_g, conv_ln_b, w_out, w_router, w_e_gate, w_e_up, w_e_down,
                 y_prompt, y_sample, new_fwd, new_bwd):
    f32, f32r, bf16, u32 = mybir.dt.float32, mybir.dt.float32r, mybir.dt.bfloat16, mybir.dt.uint32
    ALU = mybir.AluOpType
    ACT = mybir.ActivationFunctionType
    AX = mybir.AxisListType
    ctx = ExitStack()
    with ctx:
        def sb(name, shape, dt=f32):
            return ctx.enter_context(nc.sbuf_tensor(name, shape, dt))

        def sem(name):
            return ctx.enter_context(nc.semaphore(name))

        def sig(name, p, l=None):
            return Sig(sem(name), p, l)

        def dram(name, shape):
            return nc.dram_tensor(name, shape, f32, kind="Internal").ap()

        x2_rows = dram("x2_rows", (NTOK, D))
        h2_rows = dram("h2_rows", (NTOK, D + NE))
        park_q = dram("park_q", (1 + NBLK, 128, H, BT))
        park_o = dram("park_o", (1 + NBLK, 128, H, BT))
        park_r = dram("park_r", (1 + NBLK, 128, H, BT))
        park_c = dram("park_c", (1 + NBLK, 128, H, BT))
        park_s = dram("park_s", (1 + NBLK, 128, BT // CH, H * DV))

        ident = sb("ident", [128, 128])
        ones = sb("ones", [128, 128])
        ones_b = sb("ones_b", [128, 128], bf16)
        before_b = sb("before_b", [128, 128], bf16)
        keep = sb("keep", [128, 2, 128], u32)
        reset = sb("reset", [128, H * BT], bf16)
        col = sb("col", [128, 112])
        scond = sb("scond", [128, 2, 8])
        wcv = sb("wcv", [128, 4, CW])
        mod = sb("mod", [128, 48, 2])
        A1 = sb("A1", [128, 8, 2])
        A2 = sb("A2", [128, 8, 2])
        wdec = sb("wdec", [2 * RANK, H * 128])
        wr = sb("wr", [128, KC, NE])
        wz_hl = sb("wz_hl", [128, 2, KC, 2 * RANK], f32r)
        eps = sb("eps", [128, 1])
        carry = sb("carry", [128, H * DV])
        dec = sb("dec", [128, 1 + NBLK, H, BT // CH])
        logits = sb("logits", [128, NTILE, NE])
        stat = sb("stat", [128, 32])
        raw = sb("raw", [128, 2, KC, 256])
        hl = sb("hl", [128, 2, 2, KC, 256], f32r)
        act_hl = sb("act_hl", [128, 2 * 2 * KC * CAP], f32r)
        WORK = 27400
        work = sb("work", [128, WORK])
        psum = [ctx.enter_context(nc.psum_tensor(f"bank{i}", [128, 512], f32)) for i in range(8)]

        h_hl = act_hl[:, 0:2 * KC * BT].rearrange("p (s k t) -> p s k t", s=2, k=KC)
        xe_hl = act_hl[:, 0:2 * KC * CAP].rearrange("p (s k t) -> p s k t", s=2, k=KC)
        he_hl = act_hl[:, 2 * KC * CAP:4 * KC * CAP].rearrange("p (s k t) -> p s k t", s=2, k=KC)

        def carve(sizes):
            out, at = {}, 0
            for name, n in sizes:
                out[name] = work[:, at:at + n]
                at += n
            assert at <= WORK, at
            return out

        W2 = carve([("x", 2 * D), ("xn", 2 * D), ("A", H * BT), ("B", H * BT), ("C", H * BT), ("q", H * BT),
                    ("k", H * BT), ("v", 4 * 512), ("kT", 512), ("pf", 512), ("pb", 512), ("pp", 512),
                    ("oi", 2 * 512), ("S", 9 * 512), ("acc", 4 * BT), ("r", 2 * BT), ("cl", H * BT // CH)])
        W2["u"], W2["z"] = W2["q"], W2["kT"]
        vecs, w_cv = W2["A"][0:112, 0:128], W2["A"][0:CW, 128:640]
        wz = W2["A"][:, 640:640 + KC * 2 * RANK].rearrange("p (k c) -> p k c", k=KC)
        x_t = W2["x"].rearrange("p (b d) -> p b d", b=2)
        xn_t = W2["xn"].rearrange("p (b d) -> p b d", b=2)
        v_t = W2["v"].rearrange("p (t c) -> p t c", t=4)
        oi_t = W2["oi"].rearrange("p (b h t) -> p b h t", b=2, h=H)
        S_t = W2["S"].rearrange("p (n c) -> p n c", n=9)
        W3 = carve([("q", H * BT), ("o", H * BT), ("r", H * BT), ("c", H * BT), ("S", 9 * 512), ("sq", 4 * BT),
                    ("rs", 4 * BT), ("y", KC * BT), ("x", 2 * D), ("xn", 2 * D), ("h2", 2 * KC * 128)])
        S3 = W3["S"].rearrange("p (n c) -> p n c", n=9)
        sq_t = W3["sq"].rearrange("p (b t) -> p b t", b=4)
        rs_t = W3["rs"].rearrange("p (b t) -> p b t", b=4)
        x3 = W3["x"].rearrange("p (b d) -> p b d", b=2)
        xn3 = W3["xn"].rearrange("p (b d) -> p b d", b=2)
        h2T = W3["h2"].rearrange("p (b k t) -> p b k t", b=2, k=KC)
        m_t = work[:, 8192:8192 + MOD1 * KC * 256].rearrange("p (n k c) -> p n k c", n=MOD1, k=KC)
        TE = NTILE * NE
        OHR = 6
        W4 = carve([("aff", TE), ("mx", NTILE), ("sm", NTILE), ("t1", TE), ("t2", TE), ("sel", TE), ("eq", TE),
                    ("pos", TE), ("tot", TE), ("inc", TE), ("rst", TE), ("cnt", 2 * NE), ("need", 2 * NE),
                    ("thr", 2 * NE), ("cand", 2 * NE), ("bit", 2 * NE), ("kp", 2 * NE), ("kk", 2 * NE),
                    ("idf", 3 * 2), ("iota", CAPL // 2), ("mb", TE // 2), ("oh", OHR * CAPL // 2), ("idc", NTILE)])
        ids = sb("ids", [128, NE, 3], u32)
        W5 = carve([("raw2", 2 * KC * 256), ("xg", 3 * (D + NE)), ("h32", 2 * CAP), ("sg", 2 * CAP),
                    ("hx", 2 * CAP), ("yT", 4 * CAP), ("y", 3 * D), ("gate", 4)])
        xg = W5["xg"].rearrange("p (t d) -> p t d", t=3)
        h32e = W5["h32"].rearrange("p (b t) -> p b t", b=2)
        sg_t = W5["sg"].rearrange("p (b t) -> p b t", b=2)
        hx_t = W5["hx"].rearrange("p (b t) -> p b t", b=2)
        yT_t = W5["yT"].rearrange("p (b t) -> p b t", b=4)
        y_t = W5["y"].rearrange("p (t d) -> p t d", t=3)
        raw2 = W5["raw2"].rearrange("p (s k c) -> p s k c", s=2, k=KC)
        gate_t = W5["gate"]
        ids_g = sb("ids_g", [128, 3], u32)
        ids_s = sb("ids_s", [128, 3], u32)
        W6 = carve([("x", 4 * D), ("y", 4 * D), ("g", D), ("junk", D)])
        x6 = W6["x"].rearrange("p (b d) -> p b d", b=4)
        y6 = W6["y"].rearrange("p (b d) -> p b d", b=4)

        V_C, V_CTX, V_GM, V_GF, V_BM, V_CB, V_LG, V_LB, V_GN, V_BD = 0, 8, 16, 24, 32, 80, 84, 88, 92, 93
        NV = 97

        s_alone = sem("s_alone")
        s_vec = sem("s_vec")
        s_cst = sem("s_cst")
        s_vconst = sem("s_vconst")
        s_vT, s_col = sem("s_vT"), sem("s_col")
        s_silc = sem("s_silc")
        s_wz = sem("s_wz")
        s_m1 = sem("s_m1")
        s_mod = sem("s_mod")
        s_modv = sig("s_modv", 1)
        s_raw = [sem("s_raw0"), sem("s_raw1")]
        s_rawfree = [sem("s_rawfree0"), sem("s_rawfree1")]
        s_hi = sem("s_hi")
        s_lo = [sem("s_lo0"), sem("s_lo1")]
        s_unit = sem("s_unit")
        s_ph = sem("s_ph")
        s_xin = [sig("s_xin0", 16, 32), sig("s_xin1", 16, 32)]
        s_sq, s_rt, s_rstd, s_xn = sig("s_sq", 2, 4), sig("s_rt", 2, 4), sig("s_rstd", 2, 4), sig("s_xn", 2, 4)
        s_xT, s_h32, s_hhi, s_hlo = sig("s_xT", 2, 4), sig("s_h32", 2, 4), sig("s_hhi", 2, 4), sig("s_hlo", 2, 4)
        s_z, s_zt = sig("s_z", 1), sig("s_zt", 1)
        s_dec, s_abs, s_min = sig("s_dec", 4), sig("s_abs", 4), sig("s_min", 4)
        s_ln = sig("s_ln", 2)
        s_g, s_cum = sig("s_g", 1), sig("s_cum", 2)
        s_cl = sig("s_cl", 3)
        s_D = sig("s_D", 1)
        s_ex = sig("s_ex", 3)
        s_kfb, s_qfb = sig("s_kfb", 1), sig("s_qfb", 1)
        s_dk = sig("s_dk", 3)
        s_sg, s_u, s_conv = sig("s_sg", 4), sig("s_u", 4), sig("s_conv", 4 * CW)
        s_v, s_r = sig("s_v", 2), sig("s_r", 4)
        s_kt, s_kte = sig("s_kt", 2, 4), sig("s_kte", 2, 4)
        s_sf, s_sb = sig("s_sf", 2, 4), sig("s_sb", 2, 4)
        s_pf, s_pb, s_pp = sig("s_pf", 2, 4), sig("s_pb", 2, 4), sig("s_pp", 2, 4)
        s_upd, s_ue, s_fs = sig("s_upd", 4, 8), sig("s_ue", 4, 8), sig("s_fs", 4, 8)
        s_c0, s_c1 = sig("s_c0", 1), sig("s_c1", 1)
        s_oi, s_oe = sig("s_oi", 2, 4), sig("s_oe", 2, 4)
        s_qst, s_sst, s_cstr = sig("s_qst", 16), sig("s_sst", 32, 16), sig("s_cstr", 16)
        s_ost = [sig("s_ost0", 16, 32), sig("s_ost1", 16, 32)]
        s_rst = [sig("s_rst0", 32), sig("s_rst1", 32)]
        s_st = sem("s_st")
        t_q, t_o, t_r, t_c, t_S = sig("t_q", 16), sig("t_o", 16), sig("t_r", 16), sig("t_c", 16), sig("t_S", 32)
        t_x = [sig("t_x0", 16, 32), sig("t_x1", 16, 32)]
        t_c0, t_bs, t_c1 = sig("t_c0", 1), sig("t_bs", 4, 8), sig("t_c1", 1)
        t_in, t_o1, t_sq, t_ms, t_rt, t_rc, t_on, t_og, t_hi, t_lo = (
            sig("t_in", 4), sig("t_o1", 4), sig("t_sq", 4), sig("t_ms", 4), sig("t_rt", 4), sig("t_rc", 4),
            sig("t_on", 4), sig("t_og", 4), sig("t_hi", 8), sig("t_lo", 8))
        t_me, t_xc, t_csq, t_crt, t_crc, t_cn, t_si = (
            sig("t_me", 1), sig("t_xc", 4), sig("t_csq", 4), sig("t_crt", 1), sig("t_crc", 1),
            sig("t_cn", 4), sig("t_si", 4))
        t_cs = sig("t_cs", 4)
        t_y = sig("t_y", 4)
        t_yT, t_x2, t_s2, t_r2, t_i2, t_xn, t_xT, t_h2, t_ro, t_lg = (
            sig("t_yT", 2, 4), sig("t_x2", 2, 4), sig("t_s2", 2, 4), sig("t_r2", 2, 4), sig("t_i2", 2, 4),
            sig("t_xn", 2, 4), sig("t_xT", 2, 4), sig("t_h2", 2, 4), sig("t_ro", 2, 4), sig("t_lg", 2, 4))
        t_nst = sem("t_nst")
        t_x2st = [sig("t_x2st0", 16, 32), sig("t_x2st1", 16, 32)]
        t_h2st = [sig("t_h2st0", 16, 32), sig("t_h2st1", 16, 32)]
        k_v = sem("k_v")
        k_e = sem("k_e")
        k_m, k_cnt = sem("k_m"), sem("k_cnt")
        k_p = sem("k_p")
        k_oh, k_id, k_ev = sem("k_oh"), sem("k_id"), sem("k_ev")
        k_af = sem("k_af")
        e_raw = [sem(f"e_raw{i}") for i in range(4)]
        e_ids, e_gat, e_gate = sem("e_ids"), sem("e_gat"), sem("e_gate")
        e_xk, e_xh, e_xhi, e_xlo = sem("e_xk"), sem("e_xh"), sem("e_xhi"), sem("e_xlo")
        e_si, e_h, e_hhi, e_hlo = sem("e_si"), sem("e_h"), sem("e_hhi"), sem("e_hlo")
        e_yT, e_yt, e_yev, e_sc = sem("e_yT"), sem("e_yt"), sem("e_yev"), sem("e_sc")
        f_g, f_x, f_sq, f_rt, f_rc, f_y, f_st = (sem("f_g"), [sem(f"f_x{i}") for i in range(4)], sem("f_sq"),
                                                 sem("f_rt"), sem("f_rc"), sem("f_y"),
                                                 [sem(f"f_st{i}") for i in range(4)])

        def stage_end(eng, n):
            eng.drain().then_inc(s_ph, 1)
            eng.wait_ge(s_ph, 5 * n)

        block = ctx.enter_context(nc.Block())

        w_in_v = w_in[0].rearrange("(k p) c -> p k c", p=128)
        w_out_v = w_out[0].rearrange("(k p) c -> p k c", p=128)
        w_mod_v = w_mod[0].rearrange("(k p) c -> p k c", p=128)

        def slot(base, j):
            return (base + j) % 2

        def turn(base, per, i, j):
            return (base + j) // 2 + (per // 2) * i if not isinstance(i, int) or i else (base + j) // 2

        def wait_pos(eng, s, v):
            if isinstance(v, int) and v <= 0:
                return
            eng.wait_ge(s, v)

        @block.sync
        def _(sp):
            def load_unit(base, per, i, j, src):
                s = slot(base, j)
                v = turn(base, per, i, j)
                if not isinstance(v, int) or v > 0:
                    wait_alone(sp, s_alone, s_rawfree[s], v)
                sp.dma_start(raw[:, s], src).then_inc(s_raw[s], 16)

            for r, n, a in ((V_C, 8, c[0]), (V_CTX, 8, c_ctx), (V_GM, 8, norm_mix_g[0]), (V_GF, 8, norm_ffn_g[0]),
                            (V_BM, 48, b_mod[0]), (V_CB, 4, conv_b[0]), (V_LG, 4, conv_ln_g[0]),
                            (V_LB, 4, conv_ln_b[0]), (V_GN, 1, gla_norm_g[0])):
                sp.dma_start(vecs[r:r + n, :], a.rearrange("(a b) -> a b", b=128)).then_inc(s_vec, 16)
            for a, o in ((b_decay_f, 0), (b_decay_b, 64)):
                sp.dma_start(vecs[V_BD:V_BD + 4, o:o + 64], a[0].rearrange("(h k) -> h k", h=H)).then_inc(s_vec, 16)
            sp.dma_start(w_cv[:, :], conv_w[0]).then_inc(s_vec, 16)
            sp.dma_start(wr[:, :, :], w_router[0].rearrange("(k p) e -> p k e", p=128)).then_inc(s_vec, 16)
            sp.dma_start(wz[:, :, :], w_in_v[:, :, OZ:OZ + 2 * RANK]).then_inc(s_vec, 16)
            sp.wait_ge(s_cst, 4)
            for a, r, o in ((w_decay_f, 0, 0), (w_decay_b, RANK, 64)):
                sp.dma_start(wdec[r:r + RANK, :].rearrange("r (h c) -> r h c", h=H)[:, :, o:o + 64],
                             a[0].rearrange("r (h k) -> r h k", h=H)).then_inc(s_vec, 16)
            for j in range(MOD1):
                sp.dma_start(m_t[:, j], w_mod_v[:, :, 256 * j:256 * j + 256]).then_inc(s_m1, 16)
            sp.dma_start(carry[0:64, :].rearrange("k (h v) -> k h v", h=H),
                         state_gla_fwd[0, 0].rearrange("h k v -> k h v")).then_inc(s_st, 16)
            sp.dma_start(carry[64:128, :].rearrange("k (h v) -> k h v", h=H),
                         state_gla_bwd[0, 0].rearrange("h k v -> k h v")).then_inc(s_st, 16)

            def load_x(b, t):
                x_src = x_prompt[0] if b.prompt else x_sample[0].rearrange("(n t) d -> n t d", t=BT)[b.i]
                b.wait(sp, s_xn, t - 1)
                sp.dma_start(x_t[:, t % 2, :], x_src[128 * t:128 * t + 128, :]).then_inc(s_xin[t % 2].sem, 16)

            def load_proj(b, j):
                base, per = RAW_OF[SPL_PROJ_P if b.prompt else SPL_PROJ_L]
                load_unit(base, per, b.i, j, w_in_v[:, :, PROJ_COLS[j]:PROJ_COLS[j] + 256])

            def stage2(b, nb):
                n = 0 if b.prompt else b.i + 1
                for j in range(2, NPROJ):
                    load_proj(b, j)
                    if j == 4:
                        b.wait(sp, s_dk, 3)
                        sp.dma_start(park_q[n, :, :, 0:b.T],
                                     W2["B"][:, 0:H * b.T].rearrange("p (h t) -> p h t", h=H)).then_inc(s_qst.sem, 16)
                if nb is not None:
                    load_x(nb, 0)
                    load_x(nb, 1)
                if not b.prompt:
                    src = w_mod_v[:, :, 256 * MOD1:].rearrange("p k (n c) -> n p k c", n=NBLK)[b.i]
                    base, per = RAW_OF[SPL_PROJ_L]
                    for m in range(MODB):
                        if m < 2:
                            load_unit(base, per, b.i, NPROJ + m, src[:, :, 256 * m:256 * m + 256])
                for rt in range(4):
                    b.wait(sp, s_r, rt + 1)
                    sp.dma_start(park_r[n, :, rt, 0:b.T], W2["r"][:, (rt % 2) * BT:(rt % 2) * BT + b.T])\
                      .then_inc(s_rst[rt % 2].sem, 16)
                for t in range(b.NT):
                    b.wait(sp, s_oe, t + 1)
                    sp.dma_start(park_o[n, :, :, 128 * t:128 * t + 128], oi_t[:, t % 2]).then_inc(s_ost[t % 2].sem, 16)
                if nb is not None:
                    load_x(nb, 2)
                    load_x(nb, 3)
                if not b.prompt:
                    for m in range(2, MODB):
                        load_unit(base, per, b.i, NPROJ + m, src[:, :, 256 * m:256 * m + 256])
                b.wait(sp, s_fs, b.NC)
                b.wait(sp, s_ue, b.NC)
                sp.dma_start(park_s[n, :, 0:b.NC, :], S_t[:, 0:b.NC, :]).then_inc(s_sst.sem, 16)
                if b.prompt:
                    sp.dma_start(new_fwd[0, 0].rearrange("h k v -> k h v"),
                                 S_t[0:64, b.NC, :].rearrange("k (h v) -> k h v", h=H)).then_inc(s_sst.sem, 16)
                b.wait(sp, s_conv, 4 * CW)
                sp.dma_start(park_c[n, :, :, 0:b.T],
                             W2["acc"][:, 0:4 * b.T].rearrange("p (h t) -> p h t", h=4)).then_inc(s_cstr.sem, 16)
                if nb is not None:
                    load_proj(nb, 0)
                    load_proj(nb, 1)

            def stage2_done(q, b):
                for s in (s_qst, s_sst, s_cstr, *s_ost, *s_rst):
                    q.wait_ge(s.sem, b.at(s, s.p if b.prompt else s.l))

            def stage3_loads(b):
                n = 0 if b.prompt else NBLK - b.i
                for src, name, sg_, use, cnt in ((park_q, "q", t_q, t_in, 0), (park_o, "o", t_o, t_lo, 0),
                                                 (park_r, "r", t_r, t_og, 0), (park_c, "c", t_c, t_lo, 0)):
                    b.wait(sp, use, cnt)
                    sp.dma_start(W3[name][:, 0:H * b.T].rearrange("p (h t) -> p h t", h=H),
                                 src[n, :, :, 0:b.T]).then_inc(sg_.sem, 16)
                    if name == "q":
                        b.wait(sp, t_c1, 0)
                        if not b.prompt:
                            sp.wait_ge(t_nst, 16)
                        sp.dma_start(S3[0:64, 1:b.NC + 1, :], park_s[n, 0:64, 0:b.NC, :]).then_inc(t_S.sem, 16)
                        sp.dma_start(S3[64:128, 0:b.NC, :], park_s[n, 64:128, 0:b.NC, :]).then_inc(t_S.sem, 16)

            def load_out(b, j):
                base, per = RAW_OF[SPL_OUT_P if b.prompt else SPL_OUT_L]
                load_unit(base, per, b.i, j, w_out_v[:, :, 256 * j:256 * j + 256])

            def stage3(b, nb):
                if nb is not None:
                    stage3_loads(nb)
                load_out(b, 2)
                load_out(b, 3)
                x_src = x_prompt[0] if b.prompt else x_sample[0].rearrange("(n t) d -> n t d", t=BT)[NBLK - 1 - b.i]
                row = x2_rows[0:TP] if b.prompt else \
                    x2_rows[TP:NTOK].rearrange("(n t) d -> n t d", t=BT)[NBLK - 1 - b.i]
                hrow = h2_rows[0:TP] if b.prompt else \
                    h2_rows[TP:NTOK].rearrange("(n t) d -> n t d", t=BT)[NBLK - 1 - b.i]

                def load_x3(t):
                    b.wait(sp, t_x2st[t % 2], 16 * (t // 2))
                    b.wait(sp, t_xn, max(t - 1, 0))
                    sp.dma_start(x3[:, t % 2, :], x_src[128 * t:128 * t + 128, :]).then_inc(t_x[t % 2].sem, 16)

                load_x3(0)
                load_x3(1)
                if nb is not None:
                    load_out(nb, 0)
                    load_out(nb, 1)
                for t in range(b.NT):
                    b.wait(sp, t_x2, t + 1)
                    sp.dma_start(row[128 * t:128 * t + 128, :], x3[:, t % 2, :]).then_inc(t_x2st[t % 2].sem, 16)
                    b.wait(sp, t_xn, t + 1)
                    sp.dma_start(hrow[128 * t:128 * t + 128, 0:D], xn3[:, t % 2, :]).then_inc(t_h2st[t % 2].sem, 16)
                    if t + 2 < b.NT:
                        load_x3(t + 2)

            p, first, final = Blk(), Blk(0), Blk(NBLK - 1)
            load_x(p, 0)
            load_x(p, 1)
            load_proj(p, 0)
            load_proj(p, 1)
            stage2(p, first)
            with sp.Fori(0, NBLK - 1) as i:
                stage2(Blk(i, s_alone), Blk(i + 1, s_alone))
            stage2(final, None)
            stage2_done(sp, final)
            stage_end(sp, 1)
            stage3_loads(p)
            load_out(p, 0)
            load_out(p, 1)
            p.wait(sp, t_bs, p.NC)
            sp.dma_start(new_bwd[0, 0].rearrange("h k v -> k h v"),
                         S3[64:128, 0, :].rearrange("k (h v) -> k h v", h=H)).then_inc(t_nst, 16)
            stage3(p, first)
            with sp.Fori(0, NBLK - 1) as i:
                stage3(Blk(i, s_alone), Blk(i + 1, s_alone))
            stage3(final, None)
            for q in (*t_x2st, *t_h2st):
                sp.wait_ge(q.sem, final.at(q, q.l))
            stage_end(sp, 2)
            sp.wait_ge(k_v, 5)
            sp.dma_start(h2_rows[:, D:D + NE].rearrange("(t p) e -> p t e", p=128),
                         W4["aff"].rearrange("p (t e) -> p t e", e=NE)).then_inc(k_af, 16)
            sp.wait_ge(k_af, 16)
            stage_end(sp, 3)

            def expert_units(e):
                for j in range(NEXP):
                    s = j % 4
                    if j < 8:
                        src = (w_e_gate if j % 2 == 0 else w_e_up)[0, e]
                        o = 256 * (j // 2)
                    else:
                        src, o = w_e_down[0, e], 256 * (j - 8)
                    wait_alone(sp, s_alone, s_lo[j % 2], 2 * ((SPL_EXP + j - 4) // 2 + 1) + NEXP * e)
                    dst = raw[:, s] if s < 2 else raw2[:, s - 2]
                    sp.dma_start(dst, src.rearrange("(k p) c -> p k c", p=128)[:, :, o:o + 256]).then_inc(e_raw[s], 16)

            with sp.Fori(0, NE) as e:
                expert_units(e)
            stage_end(sp, 4)
            sp.dma_start(W6["g"], norm_final_g.partition_broadcast(128)).then_inc(f_g, 16)
            for t in range(NTILE + 2):
                if t < NTILE:
                    if t >= 4:
                        sp.wait_ge(f_y, t - 3)
                    sp.dma_start(x6[:, t % 4, :], x2_rows[128 * t:128 * t + 128, :]).then_inc(f_x[t % 4], 16)
                if t >= 2:
                    u = t - 2
                    sp.wait_ge(f_y, u + 1)
                    dst = y_prompt[0, 128 * u:128 * u + 128, :] if u < TP // 128 else \
                        y_sample[0, 128 * u - TP:128 * u - TP + 128, :]
                    sp.dma_start(dst, y6[:, u % 4, :]).then_inc(f_st[u % 4], 16)
            for q in range(4):
                sp.wait_ge(f_st[q], 16 * len(range(q, NTILE, 4)))

        @block.scalar
        def _(act):
            def hi_halves(base, per, i, j):
                n = base + j
                rb, rper = RAW_OF[base]
                s = slot(rb, j)
                assert s == n % 2
                act.wait_ge(s_raw[s], 16 * (turn(rb, rper, i, j) + 1))
                wait_pos(act, s_unit, per * i + (n - 1) if not isinstance(i, int) or i else n - 1)
                for q in range(2):
                    act.activation(hl[:, s, 0, :, 128 * q:128 * q + 128], raw[:, s, :, 128 * q:128 * q + 128],
                                   ACT.Copy).then_inc(s_hi, 1)

            act.wait_ge(s_cst, 20)
            act.wait_ge(s_col, 1)
            act.activation(scond[:, 0, :], col[:, V_CTX:V_CTX + 8], ACT.Silu)
            act.activation(scond[:, 1, :], col[:, V_C:V_C + 8], ACT.Silu).then_inc(s_silc, 1)
            act.wait_ge(s_vec, 16 * 16)
            act.activation(wz_hl[:, 0], wz[:, :, :], ACT.Copy).then_inc(s_wz, 1)

            def unit_done(b, base, per, j):
                act.wait_ge(s_unit, per * b.i + (base + j + 1) if not b.prompt else base + j + 1)

            def x_norm(b, t):
                b.wait(act, s_xin[t % 2], 16 * (t // 2 + 1))
                b.wait(act, s_hlo, t - 1)
                act.activation(xn_t[:, t % 2, :], x_t[:, t % 2, :], ACT.Square,
                               accum_out=stat[:, t:t + 1]).then_inc(s_sq.sem, 1)
                b.wait(act, s_sq, t + 1)
                act.activation(stat[:, 4 + t:5 + t], stat[:, t:t + 1], ACT.Sqrt, bias=eps[:, :], scale=1.0 / D)\
                   .then_inc(s_rt.sem, 1)
                b.wait(act, s_rstd, t + 1)
                act.activation(xn_t[:, t % 2, :], x_t[:, t % 2, :], ACT.Copy, scale=stat[:, 8 + t:9 + t])\
                   .then_inc(s_xn.sem, 1)

            def x_rest(nb, done):
                for t in range(done, nb.NT):
                    if t >= 2:
                        hi_tile(nb, t - 2)
                    x_norm(nb, t)
                hi_tile(nb, nb.NT - 2)
                hi_tile(nb, nb.NT - 1)

            def stage2(b, nb):
                base = SPL_PROJ_P if b.prompt else SPL_PROJ_L
                n = 0 if b.prompt else b.i + 1
                T = b.T
                hi_halves(base, NPROJ, b.i, 0)
                hi_halves(base, NPROJ, b.i, 1)
                b.wait(act, s_upd, 0)
                b.wait(act, s_z, 1)
                act.activation(W2["z"][0:2 * RANK, 0:T], psum[4][0:2 * RANK, 0:T], ACT.Copy).then_inc(s_zt.sem, 1)
                copies(b, base, 0, "k", 1.0, s_kfb, s_dk)
                hi_halves(base, NPROJ, b.i, 2)
                b.wait(act, s_qst, 0)
                for h in range(H):
                    b.wait(act, s_min, h + 1)
                    act.activation(W2["B"][:, h * T:(h + 1) * T], psum[4 + h][:, 0:T], ACT.Abs,
                                   bias=col[:, V_BD + h:V_BD + h + 1]).then_inc(s_abs.sem, 1)
                b.wait(act, s_abs, 4)
                act.activation(W2["B"][:, 0:H * T], W2["B"][:, 0:H * T], ACT.Exp, scale=-1.0).then_inc(s_ln.sem, 1)
                b.wait(act, s_ln, 1)
                act.activation(W2["B"][:, 0:H * T], W2["B"][:, 0:H * T], ACT.Ln, bias=1.0).then_inc(s_ln.sem, 1)
                copies(b, base, 1, "q", DK ** -0.5, s_qfb, s_dk)
                hi_halves(base, NPROJ, b.i, 3)
                b.wait(act, s_cum, 2)
                b.wait(act, s_g, 1)
                act.activation(W2["B"][:, 0:H * T], W2["C"][:, 0:H * T], ACT.Exp, scale=1.0 / TAU).then_inc(s_ex.sem, 1)
                b.wait(act, s_cl, 2)
                act.activation(dec[:, n, :, 0:b.NC], W2["cl"][:, 0:H * b.NC].rearrange("p (h c) -> p h c", h=H),
                               ACT.Exp, scale=1.0 / TAU).then_inc(s_D.sem, 1)
                b.wait(act, s_cl, 3)
                act.activation(W2["A"][:, 0:H * T], W2["A"][:, 0:H * T], ACT.Exp, scale=1.0 / TAU).then_inc(s_ex.sem, 1)
                act.activation(W2["C"][:, 0:H * T], W2["C"][:, 0:H * T], ACT.Exp, scale=-1.0 / TAU)\
                   .then_inc(s_ex.sem, 1)
                unit_done(b, base, NPROJ, 2)
                hi_halves(base, NPROJ, b.i, 4)
                sigmoids(b, base, 3, 0)
                hi_halves(base, NPROJ, b.i, 5)
                unit_done(b, base, NPROJ, 4)
                hi_halves(base, NPROJ, b.i, 6)
                sigmoids(b, base, 5, 2)
                hi_halves(base, NPROJ, b.i, 7)
                values(b, base, 6)
                hi_halves(base, NPROJ, b.i, 8)
                values(b, base, 7)
                hi_halves(base, NPROJ, b.i, 9)
                gla(b, 0)
                gates(b, base, 8, 0)
                gla(b, 1)
                gates(b, base, 9, 2)
                for t in range(2, b.NT):
                    if nb is not None:
                        x_norm(nb, t - 2)
                    gla(b, t)
                if nb is not None:
                    x_rest(nb, b.NT - 2)

            def hi_tile(b, t):
                b.wait(act, s_h32, t + 1)
                act.activation(h_hl[:, 0, :, 128 * t:128 * t + 128],
                               xn_t[:, t % 2, :].rearrange("p (k t) -> p k t", k=KC), ACT.Copy).then_inc(s_hhi.sem, 1)

            def copies(b, base, j, name, scale, done, used):
                unit_done(b, base, NPROJ, j)
                b.wait(act, used, 0)
                if name == "q":
                    b.wait(act, s_conv, 0)
                for h in range(H):
                    for q in range(2):
                        last = act.activation(W2[name][64 * q:64 * q + 64, h * b.T:(h + 1) * b.T],
                                              psum[2 * (j % 2) + h // 2][64 * (h % 2):64 * (h % 2) + 64, 0:b.T],
                                              ACT.Copy, scale=scale)
                last.then_inc(done.sem, 1)

            def sigmoids(b, base, j, ct):
                unit_done(b, base, NPROJ, j)
                for q in range(2):
                    b.wait(act, s_dk, 3)
                    act.activation(W2["u"][:, (ct + q) * BT:(ct + q) * BT + b.T], psum[2 * (j % 2) + q][:, 0:b.T],
                                   ACT.Sigmoid).then_inc(s_sg.sem, 1)

            def values(b, base, j):
                unit_done(b, base, NPROJ, j)
                b.wait(act, s_oi, 0)
                for q in range(b.NT // 2):
                    last = act.activation(v_t[:, 2 * q:2 * q + 2, 256 * (j - 6):256 * (j - 6) + 256],
                                          psum[2 * (j % 2) + q][:, :].rearrange("p (t c) -> p t c", t=2), ACT.Copy)
                last.then_inc(s_v.sem, 1)

            def gates(b, base, j, rt):
                unit_done(b, base, NPROJ, j)
                for q in range(2):
                    b.wait(act, s_rst[(rt + q) % 2], 16 * ((rt + q) // 2))
                    act.activation(W2["r"][:, ((rt + q) % 2) * BT:((rt + q) % 2) * BT + b.T],
                                   psum[2 * (j % 2) + q][:, 0:b.T], ACT.Silu).then_inc(s_r.sem, 1)

            def gla(b, t):
                b.wait(act, s_kt, t + 1)
                b.wait(act, s_upd, 2 * t)
                act.activation(W2["kT"][:, :], psum[4][:, :], ACT.Copy).then_inc(s_kte.sem, 1)
                if t == 0:
                    b.wait(act, s_sst, 0)
                    b.wait(act, s_c1, 0)
                for q in range(2):
                    cc = 2 * t + q
                    b.wait(act, s_upd, cc + 1)
                    act.activation(S_t[64:128, cc, :], psum[4 + q][64:128, :], ACT.Copy)
                    act.activation(S_t[0:64, cc + 1, :], psum[4 + q][0:64, :], ACT.Copy).then_inc(s_ue.sem, 1)
                b.wait(act, s_oi, t + 1)
                b.wait(act, s_ost[t % 2], 16 * (t // 2))
                act.activation(oi_t[:, t % 2], psum[7][:, :].rearrange("p (h t) -> p h t", h=H), ACT.Copy)\
                   .then_inc(s_oe.sem, 1)

            def squares(b):
                for h in range(H):
                    b.wait(act, t_o1, h + 1)
                    if h == 0:
                        b.wait(act, t_cs, 0)
                    act.activation(sq_t[:, h, 0:b.T], W3["o"][:, h * b.T:(h + 1) * b.T], ACT.Square)\
                       .then_inc(t_sq.sem, 1)

            def roots(b):
                for h in range(H):
                    b.wait(act, t_ms, h + 1)
                    if h == 0:
                        b.wait(act, t_cn, 0)
                    act.activation(rs_t[:, h, 0:b.T], psum[4 + h][:, 0:b.T], ACT.Sqrt, bias=eps[:, :], scale=1.0 / DV)\
                       .then_inc(t_rt.sem, 1)

            def conv_squares(b):
                for ct in range(4):
                    b.wait(act, t_xc, ct + 1)
                    act.activation(sq_t[:, ct, 0:b.T], W3["c"][:, ct * b.T:(ct + 1) * b.T], ACT.Square)\
                       .then_inc(t_csq.sem, 1)

            def conv_out(b):
                b.wait(act, t_cs, 4)
                b.wait(act, t_on, 4)
                act.activation(rs_t[:, 0, 0:b.T], psum[5][:, 0:b.T], ACT.Sqrt, bias=eps[:, :], scale=1.0 / 512)\
                   .then_inc(t_crt.sem, 1)
                for ct in range(4):
                    b.wait(act, t_cn, ct + 1)
                    act.activation(W3["c"][:, ct * b.T:(ct + 1) * b.T], W3["c"][:, ct * b.T:(ct + 1) * b.T], ACT.Silu,
                                   scale=col[:, V_LG + ct:V_LG + ct + 1],
                                   bias=col[:, V_LB + ct:V_LB + ct + 1]).then_inc(t_si.sem, 1)

            def cat_his(b, k0, k1):
                for k in range(k0, k1):
                    cat_hi(b, k, "o" if k < 4 else "c", t_og if k < 4 else t_si, k % 4 + 1)

            def out_copy(b, base, j):
                act.wait_ge(s_unit, NOUT * b.i + (base + j + 1) if not b.prompt else base + j + 1)
                if j == 0:
                    b.wait(act, t_yT, 0)
                for q in range(2):
                    d = 2 * j + q
                    last = act.activation(W3["y"][:, d * b.T:(d + 1) * b.T], psum[2 * (j % 2) + q][:, 0:b.T], ACT.Copy,
                                          scale=mod[:, 16 + d, b.cond:b.cond + 1])
                last.then_inc(t_y.sem, 1)

            def stage3(b, nb):
                base = SPL_OUT_P if b.prompt else SPL_OUT_L
                hi_halves(base, NOUT, b.i, 2)
                out_copy(b, base, 0)
                if nb is not None:
                    squares(nb)
                hi_halves(base, NOUT, b.i, 3)
                out_copy(b, base, 1)
                if nb is not None:
                    roots(nb)
                out_copy(b, base, 2)
                if nb is not None:
                    nbase = SPL_OUT_L
                    hi_halves(nbase, NOUT, nb.i, 0)
                    conv_squares(nb)
                out_copy(b, base, 3)
                if nb is not None:
                    hi_halves(nbase, NOUT, nb.i, 1)
                    conv_out(nb)
                per = 8 // b.NT
                for t in range(b.NT):
                    b.wait(act, t_x2, t + 1)
                    b.wait(act, t_h2st[t % 2], 16 * (t // 2))
                    b.wait(act, t_xT, max(t - 1, 0))
                    act.activation(xn3[:, t % 2, :], x3[:, t % 2, :], ACT.Square, accum_out=stat[:, t:t + 1])\
                       .then_inc(t_s2.sem, 1)
                    b.wait(act, t_s2, t + 1)
                    act.activation(stat[:, 4 + t:5 + t], stat[:, t:t + 1], ACT.Sqrt, bias=eps[:, :], scale=1.0 / D)\
                       .then_inc(t_r2.sem, 1)
                    if nb is not None:
                        cat_his(nb, per * t, per * t + per // 2)
                    b.wait(act, t_i2, t + 1)
                    act.activation(xn3[:, t % 2, :], x3[:, t % 2, :], ACT.Copy, scale=stat[:, 8 + t:9 + t])\
                       .then_inc(t_xn.sem, 1)
                    if nb is not None:
                        cat_his(nb, per * t + per // 2, per * t + per)

            def cat_hi(b, k, name, s, j):
                b.wait(act, s, j)
                o = (k % 4) * b.T
                act.activation(h_hl[:, 0, k, 0:b.T], W3[name][:, o:o + b.T], ACT.Copy).then_inc(t_hi.sem, 1)

            p, first, final = Blk(), Blk(0), Blk(NBLK - 1)
            x_rest(p, 0)
            stage2(p, first)
            with act.Fori(0, NBLK - 1) as i:
                stage2(Blk(i), Blk(i + 1))
            stage2(final, None)
            stage_end(act, 1)
            hi_halves(SPL_OUT_P, NOUT, 0, 0)
            hi_halves(SPL_OUT_P, NOUT, 0, 1)
            squares(p)
            roots(p)
            conv_squares(p)
            conv_out(p)
            cat_his(p, 0, 8)
            stage3(p, first)
            with act.Fori(0, NBLK - 1) as i:
                stage3(Blk(i), Blk(i + 1))
            stage3(final, None)
            stage_end(act, 2)
            act.wait_ge(k_v, 2)
            act.activation(W4["aff"], W4["aff"], ACT.Exp).then_inc(k_e, 1)
            stage_end(act, 3)

            def ehi(e, j):
                s = j % 4
                act.wait_ge(e_raw[s], 48 * e + 16 * (j // 4 + 1))
                act.wait_ge(s_unit, NEXP * e + (SPL_EXP + j - 1))
                src = raw[:, s] if s < 2 else raw2[:, s - 2]
                for q in range(2):
                    act.activation(hl[:, j % 2, 0, :, 128 * q:128 * q + 128], src[:, :, 128 * q:128 * q + 128],
                                   ACT.Copy).then_inc(s_hi, 1)

            def xe_hi(e, k):
                act.wait_ge(e_xh, 8 * e + (k + 1))
                act.activation(xe_hl[:, 0, k, :], h32e[:, k % 2, :], ACT.Copy).then_inc(e_xhi, 1)

            def expert(e, last):
                for j in range(NEXP):
                    if j + 2 < NEXP or not last:
                        ehi(e, j + 2)
                    act.wait_ge(s_unit, NEXP * e + (SPL_EXP + j + 1))
                    for q in range(2):
                        if j < 8 and j % 2 == 0:
                            ft = j + q
                            wait_pos(act, e_h, 8 * e + max(ft - 1, 0))
                            act.activation(sg_t[:, ft % 2, :], psum[q][:, 0:CAP], ACT.Silu).then_inc(e_si, 1)
                        elif j < 8:
                            ft = j - 1 + q
                            act.wait_ge(e_h, 8 * e + (ft + 1))
                            act.activation(he_hl[:, 0, ft, :], hx_t[:, ft % 2, :], ACT.Copy).then_inc(e_hhi, 1)
                        else:
                            d = 2 * (j - 8) + q
                            wait_pos(act, e_yt, 8 * e + max(d - 3, 0))
                            act.activation(yT_t[:, d % 4, 0:CAPL], psum[2 * (j % 2) + q][:, 0:CAPL], ACT.Copy,
                                           scale=mod[:, 40 + d, 1:2])
                            act.activation(yT_t[:, d % 4, CAPL:CAP], psum[2 * (j % 2) + q][:, CAPL:CAP], ACT.Copy,
                                           scale=mod[:, 40 + d, 0:1]).then_inc(e_yT, 1)
                    if j >= 8 and not last:
                        xe_hi(e + 1, 2 * (j - 8))
                        xe_hi(e + 1, 2 * (j - 8) + 1)

            for k in range(KC):
                xe_hi(0, k)
            ehi(0, 0)
            ehi(0, 1)
            expert(0, False)
            with act.Fori(0, NE - 2) as i:
                expert(i + 1, False)
            expert(NE - 1, True)
            stage_end(act, 4)
            for t in range(NTILE):
                act.wait_ge(f_x[t % 4], 16 * (t // 4 + 1))
                act.activation(W6["junk"], x6[:, t % 4, :], ACT.Square, accum_out=stat[:, t % 8:t % 8 + 1])\
                   .then_inc(f_sq, 1)
                act.wait_ge(f_sq, t + 1)
                if t >= 8:
                    act.wait_ge(f_rc, t - 7)
                act.activation(stat[:, 8 + t % 8:9 + t % 8], stat[:, t % 8:t % 8 + 1], ACT.Sqrt, bias=eps[:, :],
                               scale=1.0 / D).then_inc(f_rt, 1)

        @block.gpsimd
        def _(pool):
            made = [0]

            def step():
                made[0] += 1
                pool.wait_ge(s_cst, made[0])

            pool.memset(ident[:, :], 0.0).then_inc(s_cst, 1)
            step()
            pool.memset(ones[:, :], 1.0).then_inc(s_cst, 1)
            step()
            pool.memset(ones_b[:, :], 1.0).then_inc(s_cst, 1)
            step()
            pool.memset(wdec[:, :], 0.0).then_inc(s_cst, 1)
            step()
            pool.memset(reset[:, :], 1.0).then_inc(s_cst, 1)
            step()
            pool.affine_select(out=ident[:, :], in_=ident[:, :], compare_op=ALU.not_equal, fill=1.0, base=0,
                               pattern=[[-1, 128]], channel_multiplier=1).then_inc(s_cst, 1)
            step()
            pool.affine_select(out=before_b[:, :], in_=ones_b[:, :], compare_op=ALU.is_ge, fill=0.0, base=-1,
                               pattern=[[1, 128]], channel_multiplier=-1).then_inc(s_cst, 1)
            step()
            pool.memset(reset[0:64, :].rearrange("p (n t) -> p n t", t=CH)[:, :, 0:1], 0.0).then_inc(s_cst, 1)
            step()
            pool.memset(reset[64:128, :].rearrange("p (n t) -> p n t", t=CH)[:, :, CH - 1:CH], 0.0).then_inc(s_cst, 1)
            step()
            kf, kb = W2["r"][:, 0:128], W2["r"][:, BT:BT + 128]
            for m in (kf, kb):
                pool.memset(m, 1.0).then_inc(s_cst, 1)
                step()
            for m, cm, st in ((kf, -1, 1), (kb, 1, -1)):
                pool.affine_select(out=m, in_=m, compare_op=ALU.is_ge, fill=0.0, base=0,
                                   pattern=[[st, 128]], channel_multiplier=cm).then_inc(s_cst, 1)
                step()
            for m in (kf, kb):
                pool.memset(m[0:64, 64:128], 0.0).then_inc(s_cst, 1)
                step()
                pool.memset(m[64:128, 0:64], 0.0).then_inc(s_cst, 1)
                step()
            pool.tensor_copy(keep[:, 0, :], kf).then_inc(s_cst, 1)
            step()
            pool.tensor_copy(keep[:, 1, :], kb).then_inc(s_cst, 1)
            step()
            pool.memset(eps[:, :], EPS).then_inc(s_cst, 1)
            step()
            pool.wait_ge(s_wz, 1)
            pool.tensor_tensor(wz_hl[:, 1], wz[:, :, :], wz_hl[:, 0].bitcast(f32), ALU.subtract).then_inc(s_wz, 1)

            def lo_halves(base, per, i, j):
                n = base + j
                s = n % 2
                for q in range(2):
                    pool.wait_ge(s_hi, (2 * per) * i + (2 * n + q + 1) if not isinstance(i, int) or i else 2 * n + q + 1)
                    ins = pool.tensor_tensor(hl[:, s, 1, :, 128 * q:128 * q + 128], raw[:, s, :, 128 * q:128 * q + 128],
                                             hl[:, s, 0, :, 128 * q:128 * q + 128].bitcast(f32), ALU.subtract)
                    ins.then_inc(s_lo[s], 1)
                pool.wait_ge(s_lo[s], 2 * turn(base, per, i, j) + 2)
                pool.nop().then_inc(s_rawfree[s], 1)

            def lo_tile(b, t):
                b.wait(pool, s_hhi, t + 1)
                pool.tensor_tensor(h_hl[:, 1, :, 128 * t:128 * t + 128],
                                   xn_t[:, t % 2, :].rearrange("p (k t) -> p k t", k=KC),
                                   h_hl[:, 0, :, 128 * t:128 * t + 128].bitcast(f32), ALU.subtract)\
                    .then_inc(s_hlo.sem, 1)

            def stage2(b, nb):
                base = SPL_PROJ_P if b.prompt else SPL_PROJ_L
                for j in range(NPROJ):
                    lo_halves(base, NPROJ, b.i, j)
                for t in range(b.NT):
                    b.wait(pool, s_pf, t + 1)
                    b.wait(pool, s_pb, t + 1)
                    b.wait(pool, s_oi, t)
                    pool.tensor_tensor(W2["pp"], W2["pf"], W2["pb"], ALU.add).then_inc(s_pp.sem, 1)
                if nb is not None:
                    for t in range(nb.NT):
                        lo_tile(nb, t)

            def cat_lo(b):
                for k in range(8):
                    b.wait(pool, t_hi, k + 1)
                    name, o = ("o" if k < 4 else "c"), (k % 4) * b.T
                    pool.tensor_tensor(h_hl[:, 1, k, 0:b.T], W3[name][:, o:o + b.T],
                                       h_hl[:, 0, k, 0:b.T].bitcast(f32), ALU.subtract).then_inc(t_lo.sem, 1)

            def stage3(b, nb):
                base = SPL_OUT_P if b.prompt else SPL_OUT_L
                lo_halves(base, NOUT, b.i, 2)
                lo_halves(base, NOUT, b.i, 3)
                if nb is not None:
                    lo_halves(SPL_OUT_L, NOUT, nb.i, 0)
                    lo_halves(SPL_OUT_L, NOUT, nb.i, 1)
                    cat_lo(nb)

            p, first, final = Blk(), Blk(0), Blk(NBLK - 1)
            lo_tile(p, 0)
            lo_tile(p, 1)
            pool.wait_ge(s_mod, 1)
            pool.memset(W2["pf"], 0.0).then_inc(s_cst, 1)
            pool.memset(W2["pb"], 0.0).then_inc(s_cst, 1)
            stage2(p, first)
            with pool.Fori(0, NBLK - 1) as i:
                stage2(Blk(i), Blk(i + 1))
            stage2(final, None)
            stage_end(pool, 1)
            lo_halves(SPL_OUT_P, NOUT, 0, 0)
            lo_halves(SPL_OUT_P, NOUT, 0, 1)
            cat_lo(p)
            stage3(p, first)
            with pool.Fori(0, NBLK - 1) as i:
                stage3(Blk(i), Blk(i + 1))
            stage3(final, None)
            stage_end(pool, 2)
            pool.iota(W4["iota"].bitcast(bf16), [[1, CAPL]], base=0, channel_multiplier=0,
                      allow_small_or_imprecise_dtypes=True).then_inc(s_cst, 1)
            idc = W4["idc"].bitcast(bf16).rearrange("p (t c) -> p t c", c=2)
            pool.iota(idc[:, :, 0], [[1, NTILE]], base=0, channel_multiplier=0,
                      allow_small_or_imprecise_dtypes=True).then_inc(s_cst, 1)
            pool.iota(idc[:, :, 1], [[0, NTILE]], base=0, channel_multiplier=1,
                      allow_small_or_imprecise_dtypes=True).then_inc(s_cst, 1)
            stage_end(pool, 3)

            def gather(e, n_ids):
                pool.tensor_copy(ids_g[:, :], ids[:, e, :]).then_inc(e_ids, 1)
                wait_alone(pool, s_alone, e_ids, n_ids)
                for t, n in ((0, 128), (1, 128), (2, CAPP)):
                    pool.indirect_dma_start(xg[0:n, t, :], None, h2_rows[:, :],
                                            bass.IndirectOffsetOnAxis(ap=ids_g[0:n, t:t + 1], axis=0)).then_inc(e_gat, 16)

            def xe_lo(e, k):
                pool.wait_ge(e_xhi, 8 * e + (k + 1))
                pool.tensor_tensor(xe_hl[:, 1, k, :], h32e[:, k % 2, :], xe_hl[:, 0, k, :].bitcast(f32), ALU.subtract)\
                    .then_inc(e_xlo, 1)

            def expert(e, last):
                if not last:
                    pool.wait_ge(e_gat, 48 * e + 48)
                    pool.wait_ge(e_xk, 8 * e + 8)
                    pool.wait_ge(e_gate, e + 1)
                    gather(e + 1, 2 * e + 2)
                    for k in range(KC):
                        xe_lo(e + 1, k)
                wait_pos(pool, e_sc, 48 * e)
                pool.tensor_copy(ids_s[:, :], ids[:, e, :]).then_inc(e_ids, 1)
                wait_alone(pool, s_alone, e_ids, 2 * e + (2 if last else 3))
                wait_alone(pool, s_alone, e_yev, 8 * e + 8)
                for t, n in ((0, 128), (1, 128), (2, CAPP)):
                    pool.indirect_dma_start(x2_rows[:, :], bass.IndirectOffsetOnAxis(ap=ids_s[0:n, t:t + 1], axis=0),
                                            y_t[0:n, t, :], None, compute_op=ALU.add).then_inc(e_sc, 16)

            gather(0, 1)
            for k in range(KC):
                xe_lo(0, k)
            expert(0, False)
            with pool.Fori(0, NE - 2) as i:
                expert(i + 1, False)
            expert(NE - 1, True)
            pool.wait_ge(e_sc, 48 * NE)
            stage_end(pool, 4)

        @block.tensor
        def _(pe):
            pe.wait_ge(s_vec, 16 * 16)
            pe.wait_ge(s_cst, 20)
            pe.transpose(psum[0][:, 0:NV], vecs[0:NV, :], ident[0:NV, 0:NV]).then_inc(s_vT, 1)
            for ct in range(4):
                last = pe.transpose(psum[1][:, 32 * ct:32 * ct + CW], w_cv[:, 128 * ct:128 * ct + 128],
                                    ident[0:CW, 0:CW])
            last.then_inc(s_vT, 1)

            pe.wait_ge(s_silc, 1)
            pe.wait_ge(s_m1, 16 * MOD1)
            for j in range(2 * MOD1):
                for k in range(KC):
                    last = pe.matmul(psum[7][:, 2 * j:2 * j + 2], m_t[:, j // 2, k, 128 * (j % 2):128 * (j % 2) + 128],
                                     scond[:, :, k], start=(k == 0), stop=(k == KC - 1))
            last.then_inc(s_mod, 1)
            pe.wait_ge(s_wz, 2)

            def three(out, lh, ll, rh, rl, first, last_):
                pe.matmul(out, lh, rh, start=first, stop=False)
                pe.matmul(out, lh, rl, start=False, stop=False)
                return pe.matmul(out, ll, rh, start=False, stop=last_)

            def unit(base, per, b, j, cols, values=False):
                s = slot(base, j)
                T = b.T
                if values:
                    pe.wait_ge(s_lo[s], 2 * turn(base, per, b.i, j) + 2)
                    for t in range(b.NT):
                        for k in range(KC):
                            a = h_hl[:, :, k, 128 * t:128 * t + 128]
                            last = three(psum[cols + t // 2][:, 256 * (t % 2):256 * (t % 2) + 256], a[:, 0], a[:, 1],
                                         hl[:, s, 0, k, :], hl[:, s, 1, k, :], k == 0, k == KC - 1)
                else:
                    for q in range(2):
                        pe.wait_ge(s_lo[s], 2 * turn(base, per, b.i, j) + q + 1)
                        for k in range(KC):
                            w = hl[:, s, :, k, 128 * q:128 * q + 128]
                            last = three(psum[cols + q][:, 0:T], w[:, 0], w[:, 1], h_hl[:, 0, k, 0:T],
                                         h_hl[:, 1, k, 0:T], k == 0, k == KC - 1)
                last.then_inc(s_unit, 1)

            def x_T(b, pb, t):
                b.wait(pe, s_xn, t + 1)
                if t < 2:
                    if pb is not None:
                        pb.wait(pe, s_r, 2 * t + 2)
                else:
                    b.wait(pe, s_h32, t - 1)
                for k in range(KC):
                    last = pe.transpose(psum[2 * (t % 2) + k // 4][:, 128 * (k % 4):128 * (k % 4) + 128],
                                        xn_t[:, t % 2, 128 * k:128 * k + 128], ident[:, :])
                last.then_inc(s_xT.sem, 1)

            def stage2(b, nb):
                base = SPL_PROJ_P if b.prompt else SPL_PROJ_L
                T = b.T
                b.wait(pe, s_ue, 0)
                b.wait(pe, s_pb, 0)
                b.wait(pe, s_oe, 0)
                b.wait(pe, s_modv, 0 if not b.prompt else 1)
                b.wait(pe, s_hlo, b.NT)
                b.wait(pe, s_h32, b.NT)
                for k in range(KC):
                    last = three(psum[4][0:2 * RANK, 0:T], wz_hl[:, 0, k, :], wz_hl[:, 1, k, :], h_hl[:, 0, k, 0:T],
                                 h_hl[:, 1, k, 0:T], k == 0, k == KC - 1)
                last.then_inc(s_z.sem, 1)
                unit(base, NPROJ, b, 0, 0)
                b.wait(pe, s_zt, 1)
                for h in range(H):
                    pe.matmul(psum[4 + h][:, 0:T], wdec[:, 128 * h:128 * h + 128], W2["z"][0:2 * RANK, 0:T],
                              start=True, stop=True).then_inc(s_dec.sem, 1)
                unit(base, NPROJ, b, 1, 2)
                for j, (sg_, n) in enumerate(((s_kfb, 1), (s_qfb, 1), (s_u, 2), (s_sg, 2), (s_u, 4), (s_sg, 4),
                                              (s_v, 1), (s_v, 2)), 2):
                    b.wait(pe, sg_, n)
                    unit(base, NPROJ, b, j, 2 * (j % 2), values=j in (6, 7))
                    if j == 7:
                        b.wait(pe, s_abs, 4)
                        b.wait(pe, s_min, 4)
                        gla(b, 0)
                    if j == 8:
                        gla(b, 1)
                for t in range(2, b.NT):
                    if nb is not None:
                        x_T(nb, b, t - 2)
                    gla(b, t)
                if b.prompt:
                    for t in range(nb.NT):
                        x_T(nb, b, t)
                    return
                b.wait(pe, s_oe, b.NT)
                mod_units(b, 0, 2)
                if nb is not None:
                    x_T(nb, b, 2)
                mod_units(b, 2, 4)
                if nb is not None:
                    x_T(nb, b, 3)

            def mod_units(b, j0, j1):
                rb, rper = RAW_OF[SPL_PROJ_L]
                for j in range(j0, j1):
                    s = slot(rb, NPROJ + j)
                    pe.wait_ge(s_raw[s], 16 * (turn(rb, rper, b.i, NPROJ + j) + 1))
                    for q in range(2):
                        o = 2 * (2 * j + q)
                        for k in range(KC):
                            last = pe.matmul(psum[7][:, o:o + 2], raw[:, s, k, 128 * q:128 * q + 128], scond[:, :, k],
                                             start=(k == 0), stop=(k == KC - 1))
                    last.then_inc(s_rawfree[s], 1)

            def gla(b, t):
                T = b.T
                if t == 0:
                    b.wait(pe, s_dk, 3)
                b.wait(pe, s_ue, 2 * t)
                for h in range(H):
                    last = pe.transpose(psum[4][:, 128 * h:128 * h + 128],
                                        W2["A"][:, h * T + 128 * t:h * T + 128 * t + 128], ident[:, :])
                last.then_inc(s_kt.sem, 1)
                b.wait(pe, s_pb, t)
                for q, s in ((0, s_sf), (1, s_sb)):
                    for h in range(H):
                        o = h * T + 128 * t
                        last = pe.matmul(psum[5 + q][:, 128 * h:128 * h + 128],
                                         W2["C"][64 * q:64 * q + 64, o:o + 128],
                                         W2["B"][64 * q:64 * q + 64, o:o + 128], start=True, stop=True)
                    last.then_inc(s.sem, 1)
                b.wait(pe, s_kte, t + 1)
                b.wait(pe, s_v, 2)
                for q in range(2):
                    if q == 1:
                        b.wait(pe, s_pf, t + 1)
                    for h in range(H):
                        last = pe.matmul(psum[4 + q][:, 128 * h:128 * h + 128],
                                         W2["kT"][64 * q:64 * q + 64, 128 * h:128 * h + 128],
                                         v_t[64 * q:64 * q + 64, t, 128 * h:128 * h + 128], start=True, stop=True)
                    last.then_inc(s_upd.sem, 1)
                b.wait(pe, s_pp, t + 1)
                b.wait(pe, s_oe, t)
                for h in range(H):
                    last = pe.matmul(psum[7][:, 128 * h:128 * h + 128], v_t[:, t, 128 * h:128 * h + 128],
                                     W2["pp"][:, 128 * h:128 * h + 128], start=True, stop=True)
                last.then_inc(s_oi.sem, 1)

            def inter(b):
                T = b.T
                b.wait(pe, t_q, 16)
                b.wait(pe, t_S, 32)
                b.wait(pe, t_bs, b.NC)
                for h in range(H):
                    for cc in range(b.NC):
                        last = pe.matmul(psum[4 + h][:, 64 * cc:64 * cc + 64], S3[:, cc + 1, 128 * h:128 * h + 128],
                                         W3["q"][:, h * T + 64 * cc:h * T + 64 * cc + 64], start=True, stop=True)
                    last.then_inc(t_in.sem, 1)

            def square_sums(b):
                for h in range(H):
                    b.wait(pe, t_sq, h + 1)
                    pe.matmul(psum[4 + h][:, 0:b.T], ones[:, :], sq_t[:, h, 0:b.T], start=True, stop=True)\
                        .then_inc(t_ms.sem, 1)

            def conv_mean(b):
                b.wait(pe, t_c, 16)
                b.wait(pe, t_rt, 1)
                for ct in range(4):
                    last = pe.matmul(psum[4][:, 0:b.T], ones[:, :], W3["c"][:, ct * b.T:(ct + 1) * b.T],
                                     start=(ct == 0), stop=(ct == 3))
                last.then_inc(t_me.sem, 1)

            def conv_var(b):
                b.wait(pe, t_rt, 2)
                for ct in range(4):
                    b.wait(pe, t_csq, ct + 1)
                    last = pe.matmul(psum[5][:, 0:b.T], ones[:, :], sq_t[:, ct, 0:b.T], start=(ct == 0),
                                     stop=(ct == 3))
                    last.then_inc(t_cs.sem, 1)

            def stage3(b, nb):
                base = SPL_OUT_P if b.prompt else SPL_OUT_L
                T = b.T
                b.wait(pe, t_lo, 8)
                b.wait(pe, t_lg, 0)
                b.wait(pe, t_y, 0)
                unit(base, NOUT, b, 0, 0)
                if nb is not None:
                    inter(nb)
                unit(base, NOUT, b, 1, 2)
                if nb is not None:
                    square_sums(nb)
                b.wait(pe, t_y, 1)
                unit(base, NOUT, b, 2, 0)
                if nb is not None:
                    conv_mean(nb)
                b.wait(pe, t_y, 2)
                unit(base, NOUT, b, 3, 2)
                if nb is not None:
                    conv_var(nb)
                    nb.wait(pe, t_rt, 4)
                    nb.wait(pe, t_crt, 1)
                    nb.wait(pe, t_xc, 4)
                b.wait(pe, t_y, 4)

                def y_T(t):
                    b.wait(pe, t_x2, t)
                    for d in range(KC):
                        last = pe.transpose(psum[4 + d // 4][:, 128 * (d % 4):128 * (d % 4) + 128],
                                            W3["y"][:, d * T + 128 * t:d * T + 128 * t + 128], ident[:, :])
                    last.then_inc(t_yT.sem, 1)

                y_T(0)
                for t in range(b.NT):
                    if t + 1 < b.NT:
                        y_T(t + 1)
                    b.wait(pe, t_xn, t + 1)
                    b.wait(pe, t_h2, t)
                    for d in range(KC):
                        last = pe.transpose(psum[6 + d // 4][:, 128 * (d % 4):128 * (d % 4) + 128],
                                            xn3[:, t % 2, 128 * d:128 * d + 128], ident[:, :])
                    last.then_inc(t_xT.sem, 1)
                    b.wait(pe, t_h2, t + 1)
                    b.wait(pe, t_lg, max(t - 1, 0))
                    for k in range(KC):
                        last = pe.matmul(psum[t % 2][:, 0:NE], h2T[:, t % 2, k, :], wr[:, k, :], start=(k == 0),
                                         stop=(k == KC - 1))
                    last.then_inc(t_ro.sem, 1)

            p, first, final = Blk(), Blk(0), Blk(NBLK - 1)
            x_T(p, None, 0)
            x_T(p, None, 1)
            stage2(p, first)
            with pe.Fori(0, NBLK - 1) as i:
                stage2(Blk(i), Blk(i + 1))
            stage2(final, None)
            stage_end(pe, 1)
            inter(p)
            square_sums(p)
            conv_mean(p)
            conv_var(p)
            stage3(p, first)
            with pe.Fori(0, NBLK - 1) as i:
                stage3(Blk(i), Blk(i + 1))
            stage3(final, None)
            stage_end(pe, 2)
            mb = W4["mb"].bitcast(bf16)
            with pe.Fori(0, 30) as i:
                pe.wait_ge(k_m, i + 1)
                pe.matmul(psum[0][:, 0:TE], ones_b[:, :], mb, start=True, stop=True).then_inc(k_cnt, 1)
            for n in range(2):
                pe.wait_ge(k_m, 31 + n)
                pe.matmul(psum[1][:, 0:TE], ones_b[:, :], mb, start=True, stop=True)
                pe.matmul(psum[2][:, 0:TE], before_b[:, :], mb, start=True, stop=True).then_inc(k_p, 1)
            idc = W4["idc"].bitcast(bf16).rearrange("p (t c) -> p t c", c=2)
            oh = W4["oh"].bitcast(bf16).rearrange("p (b s) -> p b s", b=OHR)
            with pe.Fori(0, NE) as e:
                for t in range(NTILE):
                    pe.wait_ge(k_oh, NTILE * e + (t + 1))
                    if t < 2:
                        last = pe.matmul(psum[5][0:CAPP, 0:2], oh[:, t % OHR, 0:CAPP], idc[:, t, :], start=(t == 0),
                                         stop=(t == 1))
                    else:
                        pe.matmul(psum[3][:, 0:2], oh[:, t % OHR, 0:128], idc[:, t, :], start=(t == 2),
                                  stop=(t == NTILE - 1))
                        last = pe.matmul(psum[4][:, 0:2], oh[:, t % OHR, 128:256], idc[:, t, :], start=(t == 2),
                                         stop=(t == NTILE - 1))
                    last.then_inc(k_id, 1)
            stage_end(pe, 3)

            def gather_T(e, k):
                if k == 0:
                    pe.wait_ge(e_gat, 48 * e + 48)
                wait_pos(pe, e_xh, 8 * e + max(k - 1, 0))
                for t, n in ((0, 128), (1, 128), (2, CAPP)):
                    last = pe.transpose(psum[4 + k % 2][:, 128 * t:128 * t + n], xg[0:n, t, 128 * k:128 * k + 128],
                                        ident[0:n, 0:n])
                last.then_inc(e_xk, 1)

            def out_T(e, d):
                pe.wait_ge(e_yT, 8 * e + (d + 1))
                wait_pos(pe, e_yev, 8 * e + max(d - 1, 0))
                for t, n in ((0, 128), (1, 128), (2, CAPP)):
                    last = pe.transpose(psum[6 + d % 2][0:n, 128 * t:128 * t + 128],
                                        yT_t[:, d % 4, 128 * t:128 * t + n], ident[:, :])
                last.then_inc(e_yt, 1)

            def expert(e, last_e):
                for j in range(NEXP):
                    s = j % 2
                    if j < 8:
                        rhs, bank = xe_hl, (0 if j % 2 == 0 else 2)
                    else:
                        rhs, bank = he_hl, 2 * (j % 2)
                    for q in range(2):
                        pe.wait_ge(s_lo[s], NEXP * e + (2 * ((SPL_EXP + j) // 2) + q + 1))
                        if j == 0 or j == 1:
                            wait_pos(pe, e_yT, 8 * e)
                        elif j < 8:
                            pe.wait_ge(e_si if j % 2 == 0 else e_h, 8 * e + 2 * (j // 2))
                        elif j == 8:
                            pe.wait_ge(e_si, 8 * e + 8)
                        elif j == 9:
                            pe.wait_ge(e_h, 8 * e + 8)
                        else:
                            pe.wait_ge(e_yT, 8 * e + (2 * (j - 9)))
                        for k in range(KC):
                            if j == 0 and q == 0:
                                pe.wait_ge(e_xlo, 8 * e + (k + 1))
                            if j == 8 and q == 0:
                                pe.wait_ge(e_hlo, 8 * e + (k + 1))
                            w = hl[:, s, :, k, 128 * q:128 * q + 128]
                            last = three(psum[bank + q][:, 0:CAP], w[:, 0], w[:, 1], rhs[:, 0, k, :], rhs[:, 1, k, :],
                                         k == 0, k == KC - 1)
                    last.then_inc(s_unit, 1)
                    if j >= 9:
                        out_T(e, 2 * (j - 9))
                        out_T(e, 2 * (j - 9) + 1)
                    if j >= 8 and not last_e:
                        gather_T(e + 1, 2 * (j - 8))
                        gather_T(e + 1, 2 * (j - 8) + 1)
                out_T(e, 6)
                out_T(e, 7)

            for k in range(KC):
                gather_T(0, k)
            expert(0, False)
            with pe.Fori(0, NE - 2) as i:
                expert(i + 1, False)
            expert(NE - 1, True)
            stage_end(pe, 4)

        @block.vector
        def _(dve):
            dve.wait_ge(s_cst, 20)
            dve.wait_ge(s_vT, 1)
            dve.tensor_copy(col[:, 0:NV], psum[0][:, 0:NV]).then_inc(s_col, 1)
            dve.wait_ge(s_vT, 2)
            dve.tensor_copy(wcv[:, :, :], psum[1][:, 0:128].rearrange("p (c w) -> p c w", c=4)[:, :, 0:CW])\
               .then_inc(s_col, 1)
            dve.wait_ge(s_col, 2)

            def mod_tiles(b, t0, cnt):
                if b.prompt:
                    dve.wait_ge(s_mod, 1)
                else:
                    rb, rper = RAW_OF[SPL_PROJ_L]
                    j = NPROJ + MODB - 1
                    dve.wait_ge(s_rawfree[slot(rb, j)], turn(rb, rper, b.i, j) + 1)
                bias = col[:, bass.ds(V_BM + t0, cnt)].unsqueeze(2).broadcast_to([128, cnt, 2])
                dve.tensor_tensor(mod[:, bass.ds(t0, cnt), :], psum[7][:, 0:2 * cnt].rearrange("p (t c) -> p t c", c=2),
                                  bias, ALU.add).then_inc(s_modv.sem, 1)

            def norm_scale(n, m0, g, A):
                dve.tensor_scalar(A[:, :, :], mod[:, m0:m0 + 8, :], 1.0, None, ALU.add).then_inc(s_vconst, 1)
                dve.wait_ge(s_vconst, 2 * n - 1)
                dve.tensor_tensor(A[:, :, :], A[:, :, :], col[:, g:g + 8].unsqueeze(2).broadcast_to([128, 8, 2]),
                                  ALU.mult).then_inc(s_vconst, 1)
                dve.wait_ge(s_vconst, 2 * n)

            p, first, final = Blk(), Blk(0), Blk(NBLK - 1)
            mod_tiles(p, 0, 2 * MOD1)
            p.wait(dve, s_modv, 1)
            norm_scale(1, 8, V_GM, A1)

            def x_rstd(b, t):
                b.wait(dve, s_rt, t + 1)
                dve.reciprocal(stat[:, 8 + t:9 + t], stat[:, 4 + t:5 + t]).then_inc(s_rstd.sem, 1)

            def x_rest(nb, done):
                for t in range(done, nb.NT):
                    if t >= 2:
                        modulate(nb, t - 2)
                    x_rstd(nb, t)
                modulate(nb, nb.NT - 2)
                modulate(nb, nb.NT - 1)

            def stage2(b, nb):
                T, NC = b.T, b.NC
                n = 0 if b.prompt else b.i + 1
                A, B, C = (W2[x][:, 0:H * T] for x in "ABC")
                b.wait(dve, s_kt, 0)
                for h in range(H):
                    b.wait(dve, s_dec, h + 1)
                    dve.tensor_scalar(A[:, h * T:(h + 1) * T], psum[4 + h][:, 0:T], col[:, V_BD + h:V_BD + h + 1], 0.0,
                                      ALU.add, ALU.min).then_inc(s_min.sem, 1)
                b.wait(dve, s_min, 4)
                b.wait(dve, s_ln, 2)
                dve.tensor_tensor(A, A, B, ALU.subtract).then_inc(s_g.sem, 1)
                b.wait(dve, s_g, 1)
                b.wait(dve, s_sb, 0)
                rs = reset[:, 0:H * T]
                dve.tensor_tensor_scan(C[0:64], rs[0:64], A[0:64], 0.0, ALU.mult, ALU.add).then_inc(s_cum.sem, 1)
                dve.tensor_tensor_scan(C[64:128, ::-1], rs[64:128, ::-1], A[64:128, ::-1], 0.0, ALU.mult, ALU.add)\
                   .then_inc(s_cum.sem, 1)
                b.wait(dve, s_cum, 2)
                b.wait(dve, s_D, 0)
                cl = W2["cl"][:, 0:H * NC]
                cv = C.rearrange("p (n t) -> p n t", t=CH)
                dve.tensor_copy(cl[0:64], cv[0:64, :, CH - 1]).then_inc(s_cl.sem, 1)
                dve.tensor_copy(cl[64:128], cv[64:128, :, 0]).then_inc(s_cl.sem, 1)
                b.wait(dve, s_cl, 2)
                dve.tensor_tensor(A.rearrange("p (n t) -> p n t", t=CH),
                                  cl.unsqueeze(2).broadcast_to([128, H * NC, CH]), cv, ALU.subtract)\
                   .then_inc(s_cl.sem, 1)
                b.wait(dve, s_kfb, 1)
                b.wait(dve, s_ex, 2)
                dve.tensor_tensor(A, A, W2["k"][:, 0:H * T], ALU.mult).then_inc(s_dk.sem, 1)
                b.wait(dve, s_ex, 3)
                dve.tensor_tensor(C, C, W2["k"][:, 0:H * T], ALU.mult).then_inc(s_dk.sem, 1)
                b.wait(dve, s_qfb, 1)
                dve.tensor_tensor(B, B, W2["q"][:, 0:H * T], ALU.mult).then_inc(s_dk.sem, 1)
                b.wait(dve, s_sst, 0)
                if b.prompt:
                    dve.memset(S_t[0:64, 0, :], 0.0).then_inc(s_c0.sem, 1)
                else:
                    dve.wait_ge(s_st, 32)
                    b.wait(dve, s_c1, 0)
                    dve.tensor_copy(S_t[0:64, 0, :], carry[0:64, :]).then_inc(s_c0.sem, 1)
                glu(b, 0)
                for w in range(CW // 2):
                    taps(b, 0, w)
                glu(b, 2)
                for w in range(CW // 2, CW):
                    taps(b, 0, w)
                per = -(-CW // b.NT)
                for t in range(b.NT):
                    if t >= 2 and nb is not None:
                        x_rstd(nb, t - 2)
                    gla(b, t)
                    for w in range(per * t, min(CW, per * t + per)):
                        if t == 3 and nb is not None and w % (per // 2) == 0:
                            q = (w - per * t) // (per // 2)
                            modulate(nb, q)
                            x_rstd(nb, q + 2)
                        taps(b, 1, w)
                b.wait(dve, s_fs, NC)
                if b.prompt:
                    dve.nop().then_inc(s_c1.sem, 1)
                else:
                    dve.tensor_copy(carry[0:64, :], S_t[0:64, NC, :]).then_inc(s_c1.sem, 1)
                if nb is not None and b.prompt:
                    x_rest(nb, 0)
                elif nb is not None:
                    modulate(nb, 2)
                    modulate(nb, 3)
                if not b.prompt:
                    mod_tiles(b, 2 * MOD1 + 2 * MODB * b.i, 2 * MODB)

            def modulate(b, t):
                b.wait(dve, s_xT, t + 1)
                for k in range(KC):
                    last = dve.tensor_scalar(xn_t[:, t % 2, 128 * k:128 * k + 128],
                                             psum[2 * (t % 2) + k // 4][:, 128 * (k % 4):128 * (k % 4) + 128],
                                             A1[:, k, b.cond:b.cond + 1], mod[:, k, b.cond:b.cond + 1],
                                             ALU.mult, ALU.add)
                last.then_inc(s_h32.sem, 1)

            def glu(b, ct):
                for q in range(2):
                    b.wait(dve, s_sg, ct + q + 1)
                    uu = W2["u"][:, (ct + q) * BT:(ct + q) * BT + b.T]
                    dve.tensor_tensor(uu, psum[q][:, 0:b.T], uu, ALU.mult).then_inc(s_u.sem, 1)

            ORDER = [CW // 2] + [w for w in range(CW) if w != CW // 2]

            def taps(b, pair, n):
                w = ORDER[n]
                off = w - CW // 2
                rl = b.T if b.prompt else GRID
                for q in range(2):
                    ct = 2 * pair + q
                    uu = W2["u"][:, ct * BT:ct * BT + b.T].rearrange("p (r t) -> p r t", t=rl)
                    ac = W2["acc"][:, ct * b.T:(ct + 1) * b.T].rearrange("p (r t) -> p r t", t=rl)
                    done = 2 * CW * pair + 2 * n + q
                    if n == 0:
                        b.wait(dve, s_u, ct + 1)
                        b.wait(dve, s_cstr, 0)
                        dve.tensor_scalar(ac, uu, wcv[:, ct, w:w + 1], col[:, V_CB + ct:V_CB + ct + 1], ALU.mult,
                                          ALU.add).then_inc(s_conv.sem, 1)
                        continue
                    b.wait(dve, s_conv, done - 1)
                    a0, a1 = max(0, -off), rl - max(0, off)
                    dve.scalar_tensor_tensor(out=ac[:, :, a0:a1], in0=uu[:, :, a0 + off:a1 + off],
                                             scalar=wcv[:, ct, w:w + 1], in1=ac[:, :, a0:a1], op0=ALU.mult,
                                             op1=ALU.add).then_inc(s_conv.sem, 1)

            def gla(b, t):
                n = 0 if b.prompt else b.i + 1
                for q, s, d, name in ((0, s_sf, s_pf, "pf"), (1, s_sb, s_pb, "pb")):
                    b.wait(dve, s_pp, t)
                    if t == 0:
                        dve.wait_ge(s_cst, 22)
                    wait_alone(dve, s_alone, s.sem, b.at(s, t + 1))
                    dve.copy_predicated(W2[name].rearrange("p (h i) -> p h i", h=H),
                                    keep[:, q, :].unsqueeze(1).broadcast_to([128, H, 128]),
                                    psum[5 + q][:, :].rearrange("p (h i) -> p h i", h=H)).then_inc(d.sem, 1)
                for cc in (2 * t, 2 * t + 1):
                    b.wait(dve, s_ue, cc + 1)
                    b.wait(dve, s_D, 1)
                    b.wait(dve, s_fs, cc)
                    if cc == 0:
                        b.wait(dve, s_c0, 1)
                    for h in range(H):
                        last = dve.scalar_tensor_tensor(
                            out=S_t[0:64, cc + 1, 128 * h:128 * h + 128], in0=S_t[0:64, cc, 128 * h:128 * h + 128],
                            scalar=dec[0:64, n, h, cc:cc + 1], in1=S_t[0:64, cc + 1, 128 * h:128 * h + 128],
                            op0=ALU.mult, op1=ALU.add)
                    last.then_inc(s_fs.sem, 1)

            def back_states(b):
                T, NC = b.T, b.NC
                n = 0 if b.prompt else NBLK - b.i
                b.wait(dve, t_S, 32)
                if b.prompt:
                    dve.memset(S3[64:128, NC, :], 0.0).then_inc(t_c0.sem, 1)
                else:
                    dve.tensor_copy(S3[64:128, NC, :], carry[64:128, :]).then_inc(t_c0.sem, 1)
                b.wait(dve, t_c0, 1)
                for m, cc in enumerate(reversed(range(NC))):
                    if not (b.prompt and m == 0):
                        wait_alone(dve, s_alone, t_bs.sem, b.at(t_bs, m))
                    for h in range(H):
                        last = dve.scalar_tensor_tensor(
                            out=S3[64:128, cc, 128 * h:128 * h + 128], in0=S3[64:128, cc + 1, 128 * h:128 * h + 128],
                            scalar=dec[64:128, n, h, cc:cc + 1], in1=S3[64:128, cc, 128 * h:128 * h + 128],
                            op0=ALU.mult, op1=ALU.add)
                    last.then_inc(t_bs.sem, 1)
                b.wait(dve, t_bs, NC)
                if b.prompt:
                    dve.nop().then_inc(t_c1.sem, 1)
                else:
                    dve.tensor_copy(carry[64:128, :], S3[64:128, 0, :]).then_inc(t_c1.sem, 1)

            def add_inter(b):
                b.wait(dve, t_o, 16)
                for h in range(H):
                    b.wait(dve, t_in, h + 1)
                    o = W3["o"][:, h * b.T:(h + 1) * b.T]
                    dve.tensor_tensor(o, psum[4 + h][:, 0:b.T], o, ALU.add).then_inc(t_o1.sem, 1)

            def head_norms(b):
                b.wait(dve, t_r, 16)
                for h in range(H):
                    r = rs_t[:, h, 0:b.T]
                    b.wait(dve, t_rt, h + 1)
                    dve.reciprocal(r, r).then_inc(t_rc.sem, 1)
                for h in range(H):
                    o = W3["o"][:, h * b.T:(h + 1) * b.T]
                    b.wait(dve, t_rc, h + 1)
                    dve.tensor_tensor(o, o, rs_t[:, h, 0:b.T], ALU.mult).then_inc(t_on.sem, 1)
                for h in range(H):
                    o = W3["o"][:, h * b.T:(h + 1) * b.T]
                    b.wait(dve, t_on, h + 1)
                    dve.scalar_tensor_tensor(out=o, in0=o, scalar=col[:, V_GN:V_GN + 1],
                                             in1=W3["r"][:, h * b.T:(h + 1) * b.T], op0=ALU.mult, op1=ALU.mult)\
                       .then_inc(t_og.sem, 1)

            def centre(b):
                b.wait(dve, t_c, 16)
                b.wait(dve, t_me, 1)
                for ct in range(4):
                    x = W3["c"][:, ct * b.T:(ct + 1) * b.T]
                    dve.scalar_tensor_tensor(out=x, in0=psum[4][:, 0:b.T], scalar=-1.0 / 512, in1=x, op0=ALU.mult,
                                             op1=ALU.add).then_inc(t_xc.sem, 1)

            def conv_scale(b):
                b.wait(dve, t_crt, 1)
                dve.reciprocal(rs_t[:, 0, 0:b.T], rs_t[:, 0, 0:b.T]).then_inc(t_crc.sem, 1)
                b.wait(dve, t_crc, 1)
                b.wait(dve, t_csq, 4)
                b.wait(dve, t_xc, 4)
                for ct in range(4):
                    x = W3["c"][:, ct * b.T:(ct + 1) * b.T]
                    dve.tensor_tensor(x, x, rs_t[:, 0, 0:b.T], ALU.mult).then_inc(t_cn.sem, 1)

            def prepare(b):
                back_states(b)
                add_inter(b)
                head_norms(b)
                centre(b)
                conv_scale(b)

            def stage3(b, nb):
                if nb is not None:
                    prepare(nb)

                def residual(t):
                    b.wait(dve, t_yT, t + 1)
                    b.wait(dve, t_x[t % 2], 16 * (t // 2 + 1))
                    for q in range(2):
                        last = dve.tensor_tensor(x3[:, t % 2, 512 * q:512 * q + 512], psum[4 + q][:, :],
                                                 x3[:, t % 2, 512 * q:512 * q + 512], ALU.add)
                    last.then_inc(t_x2.sem, 1)

                residual(0)
                for t in range(b.NT):
                    b.wait(dve, t_r2, t + 1)
                    dve.reciprocal(stat[:, 8 + t:9 + t], stat[:, 4 + t:5 + t]).then_inc(t_i2.sem, 1)
                    if t + 1 < b.NT:
                        residual(t + 1)
                    b.wait(dve, t_xT, t + 1)
                    b.wait(dve, t_ro, max(t - 1, 0))
                    for k in range(KC):
                        last = dve.tensor_scalar(h2T[:, t % 2, k, :],
                                                 psum[6 + k // 4][:, 128 * (k % 4):128 * (k % 4) + 128],
                                                 A2[:, k, b.cond:b.cond + 1], mod[:, 24 + k, b.cond:b.cond + 1],
                                                 ALU.mult, ALU.add)
                    last.then_inc(t_h2.sem, 1)
                    wait_alone(dve, s_alone, t_ro.sem, b.at(t_ro, t + 1))
                    gt = t if b.prompt else (NBLK - 1 - b.i) * (BT // 128) + (TP // 128 + t)
                    dst = logits[:, gt, :] if isinstance(gt, int) else logits[:, bass.ds(gt, 1), :].squeeze(1)
                    dve.tensor_copy(dst, psum[t % 2][:, 0:NE]).then_inc(t_lg.sem, 1)

            x_rest(p, 0)
            stage2(p, first)
            with dve.Fori(0, NBLK - 1) as i:
                stage2(Blk(i), Blk(i + 1))
            stage2(final, None)
            final.wait(dve, s_modv, 1)
            norm_scale(2, 32, V_GF, A2)
            stage_end(dve, 1)
            prepare(p)
            stage3(p, first)
            with dve.Fori(0, NBLK - 1) as i:
                stage3(Blk(i), Blk(i + 1))
            stage3(final, None)
            stage_end(dve, 2)

            link_n = [0]

            def link(ins):
                link_n[0] += 1
                ins.then_inc(k_v, 1)
                dve.wait_ge(k_v, link_n[0])

            def te(name):
                return W4[name].rearrange("p (t e) -> p t e", e=NE)

            aff = te("aff")
            link(dve.tensor_reduce(W4["mx"], logits[:, :, :], AX.X, ALU.max))
            link(dve.tensor_tensor(aff, logits[:, :, :], W4["mx"].unsqueeze(2).broadcast_to([128, NTILE, NE]),
                                   ALU.subtract))
            dve.wait_ge(k_e, 1)
            link(dve.tensor_reduce(W4["sm"], aff, AX.X, ALU.add))
            link(dve.reciprocal(W4["sm"], W4["sm"]))
            link(dve.tensor_tensor(aff, aff, W4["sm"].unsqueeze(2).broadcast_to([128, NTILE, NE]), ALU.mult))
            link(dve.memset(W4["kk"][:, 0:NE], float(CAPP)))
            link(dve.memset(W4["kk"][:, NE:2 * NE], float(CAPL)))
            thr, cand, bit, kp = (W4[x].bitcast(u32) for x in ("thr", "cand", "bit", "kp"))
            link(dve.memset(W4["thr"], 0.0))
            link(dve.memset(bit, 1 << 29))
            cnt, need = W4["cnt"], W4["need"]
            mb = W4["mb"].bitcast(bf16)
            PT = TP // 128
            sets = ((0, PT, 0), (PT, NTILE, 1))

            def per_set(out, op, src, values_):
                for a, z, s in sets:
                    v = values_[:, NE * s:NE * s + NE].unsqueeze(1).broadcast_to([128, z - a, NE])
                    ins = dve.tensor_tensor(out[:, a:z, :], src[:, a:z, :], v, op)
                return ins

            mb3 = mb.rearrange("p (t e) -> p t e", e=NE)
            base = link_n[0]
            PER = 5
            with dve.Fori(0, 30) as i:
                def step(j, ins):
                    ins.then_inc(k_v, 1)
                    wait_alone(dve, s_alone, k_v, PER * i + (base + j))
                step(1, dve.tensor_tensor(cand, thr, bit, ALU.bitwise_or))
                per_set(mb3, ALU.is_ge, aff, W4["cand"]).then_inc(k_m, 1)
                step(2, dve.tensor_scalar(bit, bit, 1, None, ALU.logical_shift_right))
                dve.wait_ge(k_cnt, i + 1)
                for a, z, s in sets:
                    ins = dve.tensor_reduce(cnt[:, NE * s:NE * s + NE],
                                            psum[0][:, NE * a:NE * z].rearrange("p (t e) -> p e t", e=NE), AX.X,
                                            ALU.add)
                step(3, ins)
                step(4, dve.tensor_tensor(kp, cnt, W4["kk"], ALU.is_ge))
                step(5, dve.copy_predicated(thr, kp, cand))
            link_n[0] = base + PER * 30
            per_set(te("sel"), ALU.is_gt, aff, W4["thr"])
            link(per_set(te("eq"), ALU.is_equal, aff, W4["thr"]))

            rst = W4["rst"].rearrange("p (e t) -> p e t", e=NE)
            link(dve.memset(W4["rst"], 1.0))
            dve.memset(rst[:, :, 0:1], 0.0)
            link(dve.memset(rst[:, :, PT:PT + 1], 0.0))
            tot, inc = W4["tot"], W4["inc"]

            def rank(out, n):
                dve.wait_ge(k_p, n)
                link(dve.tensor_copy(tot.rearrange("p (e t) -> p e t", e=NE),
                                     psum[1][:, 0:TE].rearrange("p (t e) -> p e t", e=NE)))
                link(dve.tensor_tensor_scan(inc, W4["rst"], tot, 0.0, ALU.mult, ALU.add))
                link(dve.tensor_tensor(inc, inc, tot, ALU.subtract))
                link(dve.tensor_tensor(out, psum[2][:, 0:TE].rearrange("p (t e) -> p t e", e=NE),
                                       inc.rearrange("p (e t) -> p t e", e=NE), ALU.add))

            dve.tensor_copy(mb, W4["eq"]).then_inc(k_m, 1)
            rank(te("pos"), 1)
            dve.tensor_copy(mb, W4["sel"]).then_inc(k_m, 1)
            dve.wait_ge(k_p, 2)
            for a, z, s in sets:
                ins = dve.tensor_reduce(cnt[:, NE * s:NE * s + NE],
                                        psum[1][:, NE * a:NE * z].rearrange("p (t e) -> p e t", e=NE), AX.X, ALU.add)
            link(ins)
            link(dve.tensor_tensor(need, W4["kk"], cnt, ALU.subtract))
            link(per_set(te("t1"), ALU.is_lt, te("pos"), need))
            link(dve.tensor_tensor(W4["t1"], W4["t1"], W4["eq"], ALU.mult))
            dve.tensor_copy(W4["t2"], W4["pos"])
            rank(te("pos"), 2)
            link(per_set(te("t2"), ALU.add, te("t2"), cnt))
            link(dve.tensor_tensor(W4["t2"], W4["t2"], W4["t1"], ALU.mult))
            link(dve.tensor_tensor(W4["pos"], W4["pos"], W4["sel"], ALU.mult))
            link(dve.tensor_tensor(W4["pos"], W4["pos"], W4["t2"], ALU.add))
            link(dve.tensor_tensor(W4["sel"], W4["sel"], W4["t1"], ALU.add))
            link(dve.tensor_scalar(W4["sel"], W4["sel"], -1.0, 4096.0, ALU.add, ALU.mult))
            link(dve.tensor_tensor(W4["pos"], W4["pos"], W4["sel"], ALU.add))
            link(dve.memset(ids[:, :, :], 0))
            dve.wait_ge(s_cst, 25)
            oh = W4["oh"].bitcast(bf16).rearrange("p (b s) -> p b s", b=OHR)
            slots = W4["iota"].bitcast(bf16)
            idf = W4["idf"].rearrange("p (t c) -> p t c", c=2)
            base2 = link_n[0]
            with dve.Fori(0, NE) as e:
                for t in range(NTILE):
                    if t >= OHR:
                        dve.wait_ge(k_id, NTILE * e + (t - OHR + 1))
                    cap = CAPP if t < PT else CAPL
                    pos_e = te("pos")[:, t, bass.ds(e, 1)]
                    dve.tensor_scalar(oh[:, t % OHR, 0:cap], slots[:, 0:cap], pos_e, None,
                                      ALU.is_equal).then_inc(k_oh, 1)
                dve.wait_ge(k_id, NTILE * e + NTILE)
                for s, n in ((0, 128), (1, 128), (2, CAPP)):
                    ins = dve.tensor_copy(idf[0:n, s, :], psum[3 + s][0:n, 0:2])
                ins.then_inc(k_ev, 1)
                dve.wait_ge(k_ev, 2 * e + 1)
                for s, n in ((0, 128), (1, 128), (2, CAPP)):
                    ins = dve.scalar_tensor_tensor(out=ids[0:n, bass.ds(e, 1), s], in0=idf[0:n, s, 0:1], scalar=128.0,
                                                   in1=idf[0:n, s, 1:2], op0=ALU.mult, op1=ALU.add)
                ins.then_inc(k_ev, 1)
                wait_alone(dve, s_alone, k_ev, 2 * e + 2)
            stage_end(dve, 3)

            def elo(e, j):
                s = j % 4
                src = raw[:, s] if s < 2 else raw2[:, s - 2]
                for q in range(2):
                    dve.wait_ge(s_hi, 2 * NEXP * e + (2 * (SPL_EXP + j) + q + 1))
                    dve.tensor_tensor(hl[:, j % 2, 1, :, 128 * q:128 * q + 128], src[:, :, 128 * q:128 * q + 128],
                                      hl[:, j % 2, 0, :, 128 * q:128 * q + 128].bitcast(f32), ALU.subtract)\
                       .then_inc(s_lo[j % 2], 1)

            def gather_mod(e, k):
                dve.wait_ge(e_xk, 8 * e + (k + 1))
                wait_pos(dve, e_xlo, 8 * e + max(k - 1, 0))
                for a, z, cnd in ((0, CAPL, 1), (CAPL, CAP, 0)):
                    last = dve.tensor_scalar(h32e[:, k % 2, a:z], psum[4 + k % 2][:, a:z], A2[:, k, cnd:cnd + 1],
                                             mod[:, 24 + k, cnd:cnd + 1], ALU.mult, ALU.add)
                last.then_inc(e_xh, 1)

            def gate_cols(e):
                dve.wait_ge(e_gat, 48 * e + 48)
                wait_pos(dve, e_yev, 8 * e)
                for s, n in ((0, 128), (1, 128), (2, CAPP)):
                    src = xg[0:n, s, D:D + NE][:, bass.ds(e, 1)] if not isinstance(e, int) else \
                        xg[0:n, s, D + e:D + e + 1]
                    last = dve.tensor_copy(gate_t[0:n, s:s + 1], src)
                last.then_inc(e_gate, 1)

            def out_rows(e, d):
                dve.wait_ge(e_yt, 8 * e + (d + 1))
                if d == 0:
                    wait_pos(dve, e_sc, 48 * e)
                    dve.wait_ge(e_gate, e + 1)
                for s, n in ((0, 128), (1, 128), (2, CAPP)):
                    last = dve.tensor_scalar(y_t[0:n, s, 128 * d:128 * d + 128],
                                             psum[6 + d % 2][0:n, 128 * s:128 * s + 128], gate_t[0:n, s:s + 1], None,
                                             ALU.mult)
                last.then_inc(e_yev, 1)

            def expert(e, last_e):
                gate_cols(e)
                for j in range(NEXP):
                    if j + 2 < NEXP or not last_e:
                        elo(e, j + 2)
                    if j < 8 and j % 2 == 1:
                        for q in range(2):
                            ft = j - 1 + q
                            dve.wait_ge(e_si, 8 * e + (ft + 1))
                            dve.wait_ge(s_unit, NEXP * e + (SPL_EXP + j + 1))
                            wait_pos(dve, e_hlo, 8 * e + max(ft - 1, 0))
                            dve.tensor_tensor(hx_t[:, ft % 2, :], psum[2 + q][:, 0:CAP], sg_t[:, ft % 2, :], ALU.mult)\
                               .then_inc(e_h, 1)
                        for q in range(2):
                            ft = j - 1 + q
                            dve.wait_ge(e_hhi, 8 * e + (ft + 1))
                            dve.tensor_tensor(he_hl[:, 1, ft, :], hx_t[:, ft % 2, :], he_hl[:, 0, ft, :].bitcast(f32),
                                              ALU.subtract).then_inc(e_hlo, 1)
                    if j >= 9:
                        out_rows(e, 2 * (j - 9))
                        out_rows(e, 2 * (j - 9) + 1)
                    if j >= 8 and not last_e:
                        gather_mod(e + 1, 2 * (j - 8))
                        gather_mod(e + 1, 2 * (j - 8) + 1)
                out_rows(e, 6)
                out_rows(e, 7)

            for k in range(KC):
                gather_mod(0, k)
            elo(0, 0)
            elo(0, 1)
            expert(0, False)
            with dve.Fori(0, NE - 2) as i:
                expert(i + 1, False)
            expert(NE - 1, True)
            stage_end(dve, 4)
            dve.wait_ge(f_g, 16)
            for t in range(NTILE):
                dve.wait_ge(f_rt, t + 1)
                dve.reciprocal(stat[:, 16 + t % 8:17 + t % 8], stat[:, 8 + t % 8:9 + t % 8]).then_inc(f_rc, 1)
                dve.wait_ge(f_rc, t + 1)
                if t >= 4:
                    dve.wait_ge(f_st[t % 4], 16 * (t // 4))
                dve.scalar_tensor_tensor(out=y6[:, t % 4, :], in0=x6[:, t % 4, :], scalar=stat[:, 16 + t % 8:17 + t % 8],
                                         in1=W6["g"], op0=ALU.mult, op1=ALU.mult).then_inc(f_y, 1)


_INS = ['x_prompt', 'x_sample', 'state_gla_fwd', 'state_gla_bwd', 'c', 'c_ctx', 'norm_mix_g', 'norm_ffn_g',
        'norm_final_g', 'w_mod', 'b_mod', 'w_in', 'w_decay_f', 'b_decay_f', 'w_decay_b', 'b_decay_b', 'gla_norm_g',
        'conv_w', 'conv_b', 'conv_ln_g', 'conv_ln_b', 'w_out', 'w_router', 'w_e_gate', 'w_e_up', 'w_e_down']
_OUTS = [((1, TP, D), 'float32'), ((1, TL, D), 'float32'), ((1, 1, H, DK, DV), 'float32'),
         ((1, 1, H, DK, DV), 'float32')]


def kernel(**inputs):
    import numpy as _np
    import concourse.bacc as _bacc
    from concourse import mybir as _mybir
    from concourse.bass_utils import run_bass_kernel_spmd as _run

    nc = _bacc.Bacc("TRN2", target_bir_lowering=False, num_devices=1)
    arrays, args = {}, []
    for name in _INS:
        a = _np.ascontiguousarray(inputs[name])
        arrays[f"in_{name}_dram"] = a
        args.append(nc.dram_tensor(f"in_{name}_dram", a.shape, _mybir.dt.from_np(a.dtype), kind="ExternalInput").ap())
    for i, (shape, dtype) in enumerate(_OUTS):
        dt = _mybir.dt.from_np(_np.dtype(dtype))
        args.append(nc.dram_tensor(f"out_{i}_dram", shape, dt, kind="ExternalOutput").ap())
    hybrid_layer(nc, *args)
    r = _run(nc, [arrays], core_ids=[0])
    return tuple(r.results[0][f"out_{i}_dram"] for i in range(len(_OUTS)))
```
